# Optimizing a Trainium2 kernel written in Bass

```python
import jax, jax.numpy as jnp
from jax import lax
import numpy as np

D_MODEL = 1024
BATCH = 1
SEQ = 1024
DEPTH = 1

CHUNK = 64
EPS = 1e-6
SSM_HEADS = 16
SSM_HEAD_DIM = 64
SSM_WIDTH = SSM_HEADS * SSM_HEAD_DIM
SSM_GROUPS = 2
D_STATE = 128
SSM_CONV = 4
XBC_WIDTH = SSM_WIDTH + 2 * SSM_GROUPS * D_STATE
ATTN_HEADS = 16
KV_HEADS = 4
HEAD_DIM = 64
ATTN_WIDTH = ATTN_HEADS * HEAD_DIM
KV_WIDTH = KV_HEADS * HEAD_DIM
WINDOW = 128
WINDOW_CHUNKS = WINDOW // CHUNK
ROPE_DIMS = HEAD_DIM // 4
ROPE_THETA = 500000.0
MIX_WIDTH = SSM_WIDTH + ATTN_WIDTH
IN_WIDTH = SSM_WIDTH + XBC_WIDTH + SSM_HEADS + ATTN_WIDTH + 2 * KV_WIDTH
D_FF = 2816
FFN_CONV = 3

kernel_name = 'hymba_ssd_swa_sink_convglu_block'

def rmsnorm(x, g):
    xf = x.astype(jnp.float32)
    y = xf * lax.rsqrt(jnp.mean(xf * xf, axis=-1, keepdims=True) + EPS)
    return (y * g.astype(jnp.float32)).astype(x.dtype)

def causal_dwconv(x, w, b):
    k, c = w.shape
    y = lax.conv_general_dilated(x, w[:, None, :], window_strides=(1,),
                                 padding=[(k - 1, 0)],
                                 dimension_numbers=('NWC', 'WIO', 'NWC'),
                                 feature_group_count=c)
    return y + b

def partial_rope(x, positions):
    half = ROPE_DIMS // 2
    inv_freq = ROPE_THETA ** (-jnp.arange(0, ROPE_DIMS, 2, dtype=jnp.float32) / ROPE_DIMS)
    ang = positions.astype(jnp.float32)[..., None] * inv_freq
    cos = jnp.cos(ang)[:, :, None, :]
    sin = jnp.sin(ang)[:, :, None, :]
    xf = x.astype(jnp.float32)
    x1 = xf[..., :half]
    x2 = xf[..., half:ROPE_DIMS]
    rot = jnp.concatenate([x1 * cos - x2 * sin, x2 * cos + x1 * sin, xf[..., ROPE_DIMS:]], axis=-1)
    return rot.astype(x.dtype)

def ssd_chunked(x, dt, a, bmat, cmat):
    b, l, h, p = x.shape
    g, n = bmat.shape[2], bmat.shape[3]
    r = h // g
    nc = l // CHUNK
    xc = x.reshape(b, nc, CHUNK, g, r, p)
    dtc = dt.reshape(b, nc, CHUNK, g, r)
    bc = bmat.reshape(b, nc, CHUNK, g, n)
    cc = cmat.reshape(b, nc, CHUNK, g, n)
    a_cs = jnp.cumsum(dtc * a.reshape(g, r), axis=2)
    causal = jnp.tril(jnp.ones((CHUNK, CHUNK), dtype=bool))[:, :, None, None]
    seg = a_cs[:, :, :, None] - a_cs[:, :, None, :]
    decay_in = jnp.exp(jnp.where(causal, seg, -jnp.inf))
    cb = jnp.einsum('bclgn,bcsgn->bclsg', cc, bc)
    w = cb[..., None] * decay_in * dtc[:, :, None]
    y_diag = jnp.einsum('bclsgr,bcsgrp->bclgrp', w, xc)
    decay_to_end = jnp.exp(a_cs[:, :, -1:] - a_cs)
    states = jnp.einsum('bcsgn,bcsgr,bcsgrp->bcgrpn', bc, decay_to_end * dtc, xc).astype(jnp.float32)
    chunk_decay = jnp.exp(a_cs[:, :, -1])

    def step(carry, inp):
        s, dec = inp
        return carry * dec[..., None, None] + s, carry

    init = jnp.zeros((b, g, r, p, n), jnp.float32)
    _, prev = lax.scan(step, init, (jnp.moveaxis(states, 1, 0), jnp.moveaxis(chunk_decay, 1, 0)))
    prev = jnp.moveaxis(prev, 0, 1)
    y_off = jnp.einsum('bclgn,bcgrpn,bclgr->bclgrp', cc, prev, jnp.exp(a_cs))
    return (y_diag + y_off).reshape(b, l, h, p)

def band_attention_with_sinks(q, k, v, sinks):
    b, l, hq, d = q.shape
    hkv = k.shape[2]
    grp = hq // hkv
    nc = l // CHUNK
    pad = (WINDOW_CHUNKS - 1) * CHUNK
    kp = jnp.pad(k, ((0, 0), (pad, 0), (0, 0), (0, 0)))
    vp = jnp.pad(v, ((0, 0), (pad, 0), (0, 0), (0, 0)))
    kb = jnp.concatenate([kp[:, j * CHUNK:j * CHUNK + l].reshape(b, nc, CHUNK, hkv, d)
                          for j in range(WINDOW_CHUNKS)], axis=2)
    vb = jnp.concatenate([vp[:, j * CHUNK:j * CHUNK + l].reshape(b, nc, CHUNK, hkv, d)
                          for j in range(WINDOW_CHUNKS)], axis=2)
    qb = q.reshape(b, nc, CHUNK, hkv, grp, d)
    scores = jnp.einsum('bcqkgd,bcskd->bkgcqs', qb, kb).astype(jnp.float32) * (HEAD_DIM ** -0.5)
    key_chunk = jnp.arange(nc)[:, None] - (WINDOW_CHUNKS - 1) + jnp.arange(WINDOW)[None, :] // CHUNK
    valid = (key_chunk >= 0)[None, None, None, :, None, :]
    scores = jnp.where(valid, scores, -jnp.inf)
    sk = sinks.astype(jnp.float32).reshape(hkv, grp)[None, :, :, None, None, None]
    m = jnp.maximum(jnp.max(scores, axis=-1, keepdims=True), sk)
    pexp = jnp.exp(scores - m)
    denom = jnp.sum(pexp, axis=-1, keepdims=True) + jnp.exp(sk - m)
    probs = (pexp / denom).astype(v.dtype)
    out = jnp.einsum('bkgcqs,bcskd->bcqkgd', probs, vb)
    return out.reshape(b, l, hq * d)

def setup_inputs(seed: int = 0) -> dict:
    key = jax.random.key(seed)
    ks = jax.random.split(key, 20)
    f32 = jnp.float32
    x = jax.random.normal(ks[0], (BATCH, SEQ, D_MODEL), f32)
    offset = jax.random.randint(ks[1], (BATCH, 1), 0, 1024) * CHUNK
    positions = (offset + jnp.arange(SEQ)[None, :]).astype(jnp.int32)
    norm_mix = 1.0 + 0.02 * jax.random.normal(ks[2], (DEPTH, D_MODEL), f32)
    w_in = jax.random.normal(ks[3], (DEPTH, D_MODEL, IN_WIDTH), f32) * D_MODEL ** -0.5
    conv_w = jax.random.normal(ks[4], (DEPTH, SSM_CONV, XBC_WIDTH), f32) * SSM_CONV ** -0.5
    conv_b = 0.02 * jax.random.normal(ks[5], (DEPTH, XBC_WIDTH), f32)
    dt0 = jnp.exp(jax.random.uniform(ks[6], (DEPTH, SSM_HEADS), f32, np.log(1e-3), np.log(1e-1)))
    dt_bias = dt0 + jnp.log(-jnp.expm1(-dt0))
    a_log = jnp.log(jax.random.uniform(ks[7], (DEPTH, SSM_HEADS), f32, 1.0, 16.0))
    d_skip = 1.0 + 0.1 * jax.random.normal(ks[8], (DEPTH, SSM_HEADS), f32)
    ssm_norm = 1.0 + 0.02 * jax.random.normal(ks[9], (DEPTH, SSM_WIDTH), f32)
    q_norm = 1.0 + 0.02 * jax.random.normal(ks[10], (DEPTH, HEAD_DIM), f32)
    k_norm = 1.0 + 0.02 * jax.random.normal(ks[11], (DEPTH, HEAD_DIM), f32)
    sinks = 0.5 * jax.random.normal(ks[12], (DEPTH, ATTN_HEADS), f32)
    w_out = jax.random.normal(ks[13], (DEPTH, MIX_WIDTH, D_MODEL), f32) * MIX_WIDTH ** -0.5
    norm_ffn = 1.0 + 0.02 * jax.random.normal(ks[14], (DEPTH, D_MODEL), f32)
    w_ffn_in = jax.random.normal(ks[15], (DEPTH, D_MODEL, 2 * D_FF), f32) * D_MODEL ** -0.5
    ffn_conv_w = jax.random.normal(ks[16], (DEPTH, FFN_CONV, D_FF), f32) * FFN_CONV ** -0.5
    ffn_conv_b = 0.02 * jax.random.normal(ks[17], (DEPTH, D_FF), f32)
    w_ffn_out = jax.random.normal(ks[18], (DEPTH, D_FF, D_MODEL), f32) * D_FF ** -0.5
    return {'x': x, 'positions': positions, 'norm_mix': norm_mix, 'w_in': w_in,
            'conv_w': conv_w, 'conv_b': conv_b, 'dt_bias': dt_bias, 'a_log': a_log,
            'd_skip': d_skip, 'ssm_norm': ssm_norm, 'q_norm': q_norm, 'k_norm': k_norm,
            'sinks': sinks, 'w_out': w_out, 'norm_ffn': norm_ffn, 'w_ffn_in': w_ffn_in,
            'ffn_conv_w': ffn_conv_w, 'ffn_conv_b': ffn_conv_b, 'w_ffn_out': w_ffn_out}

def reference(x, positions, norm_mix, w_in, conv_w, conv_b, dt_bias, a_log, d_skip,
              ssm_norm, q_norm, k_norm, sinks, w_out, norm_ffn, w_ffn_in, ffn_conv_w,
              ffn_conv_b, w_ffn_out):
    b, l, _ = x.shape
    splits = list(np.cumsum([SSM_WIDTH, XBC_WIDTH, SSM_HEADS, ATTN_WIDTH, KV_WIDTH]))
    for i in range(DEPTH):
        h = rmsnorm(x, norm_mix[i])
        proj = h @ w_in[i]
        z, xbc, dt_raw, q, k, v = jnp.split(proj, splits, axis=-1)
        xbc = jax.nn.silu(causal_dwconv(xbc, conv_w[i], conv_b[i]))
        xs, bs, cs = jnp.split(xbc, [SSM_WIDTH, SSM_WIDTH + SSM_GROUPS * D_STATE], axis=-1)
        xs = xs.reshape(b, l, SSM_HEADS, SSM_HEAD_DIM)
        dt = jax.nn.softplus(dt_raw.astype(jnp.float32) + dt_bias[i].astype(jnp.float32))
        a = -jnp.exp(a_log[i].astype(jnp.float32))
        y = ssd_chunked(xs, dt, a, bs.reshape(b, l, SSM_GROUPS, D_STATE),
                        cs.reshape(b, l, SSM_GROUPS, D_STATE))
        y = y + d_skip[i].astype(jnp.float32)[:, None] * xs
        y = y.reshape(b, l, SSM_WIDTH).astype(x.dtype)
        ssm_out = rmsnorm(y * jax.nn.silu(z), ssm_norm[i])
        q = partial_rope(rmsnorm(q.reshape(b, l, ATTN_HEADS, HEAD_DIM), q_norm[i]), positions)
        k = partial_rope(rmsnorm(k.reshape(b, l, KV_HEADS, HEAD_DIM), k_norm[i]), positions)
        v = v.reshape(b, l, KV_HEADS, HEAD_DIM)
        attn_out = band_attention_with_sinks(q, k, v, sinks[i])
        x = x + jnp.concatenate([ssm_out, attn_out], axis=-1) @ w_out[i]
        h2 = rmsnorm(x, norm_ffn[i])
        gate, val = jnp.split(h2 @ w_ffn_in[i], [D_FF], axis=-1)
        gate = causal_dwconv(gate, ffn_conv_w[i], ffn_conv_b[i])
        x = x + (jax.nn.silu(gate) * val) @ w_ffn_out[i]
    return x


_drawn_inputs = setup_inputs


def setup_inputs(seed=0):
    import zlib

    import numpy as np

    out = dict(_drawn_inputs(seed))
    spreads = {}
    factors = {'norm_mix': 2.829,
     'conv_b': 2.997,
     'ssm_norm': 4.523,
     'q_norm': 8.0,
     'k_norm': 8.0,
     'sinks': 8.0,
     'norm_ffn': 4.507,
     'ffn_conv_b': 6.382,
     'd_skip': 40.526}
    for name, (base, spread) in spreads.items():
        noise = np.random.default_rng([zlib.crc32(name.encode()), seed]).standard_normal(out[name].shape)
        drawn = base * np.exp(spread * noise) if base else spread * noise
        out[name] = __import__('jax').numpy.asarray(drawn.astype(out[name].dtype))
    for name, factor in factors.items():
        out[name] = (out[name] * factor).astype(out[name].dtype)
    return out
```

```python
from contextlib import ExitStack

import numpy as np

import concourse.bass as bass
from concourse import mybir

F32 = mybir.dt.float32
F32R = mybir.dt.float32r
I32 = mybir.dt.int32
ACT = mybir.ActivationFunctionType
ALU = mybir.AluOpType
AX = mybir.AxisListType
ds = bass.ds

P = 128
L = 1024
D = 1024
NT = L // P
NK = D // P
HALF = 512
EPS = 1e-6

SSM_H, SSM_P, SSM_G, STATE, SSM_CONV = 16, 64, 2, 128, 4
SSM_W = SSM_H * SSM_P
HPG = SSM_H // SSM_G
XBC_W = SSM_W + 2 * SSM_G * STATE
NB_XBC = XBC_W // P
Q_H, KV_H, HD = 16, 4, 64
QK_H = Q_H + KV_H
CHUNK = 64
ROPE = HD // 4
RH = ROPE // 2
THETA = 500000.0
SCALE = HD ** -0.5
Z0 = 0
XBC0 = SSM_W
DT0 = XBC0 + XBC_W
Q0 = DT0 + SSM_H
KV0 = Q0 + Q_H * HD
KV_W = KV_H * HD
IN_W = KV0 + 2 * KV_W
MIX_W = SSM_W + Q_H * HD
NM = MIX_W // P
D_FF = 2816
NF = D_FF // P
FFN_CONV = 3
GF = 2
NG = NF // GF
PB = 256
BIG = 1e30

PC_MIX, PC_FFN, PC_SSM, PC_CW = 0, NK, 2 * NK, 3 * NK
PC_CB = PC_CW + SSM_CONV * NB_XBC
PC1 = PC_CB + NB_XBC
PC_FB = FFN_CONV * NF
PC2 = PC_FB + NF

PASSES = (("hi", "hi"), ("hi", "lo"), ("lo", "hi"))


class Room:

    def __init__(self, nc, ctx, stage):
        self.nc, self.ctx, self.stage, self.sems = nc, ctx, stage, []

    def sb(self, name, shape, dt=F32):
        return self.ctx.enter_context(self.nc.sbuf_tensor(f"{self.stage}_{name}", shape, dt))

    def ps(self, name, shape):
        return self.ctx.enter_context(self.nc.psum_tensor(f"{self.stage}_{name}", shape, F32))

    def sem(self, name):
        self.sems.append(self.nc.alloc_semaphore(f"{self.stage}_{name}"))
        return self.sems[-1]

    def clear(self):
        self.nc.clear_and_free_semaphores(self.sems)
        self.nc.all_engine_barrier()


class Chain:

    def __init__(self, eng, sem, per=0):
        self.eng, self.sem, self.per, self.base, self.n = eng, sem, per, 0, 0

    def turn(self, i):
        self.base, self.n = i * self.per, 0

    def link(self, ins):
        ins.then_inc(self.sem, 1)
        self.n += 1
        self.eng.wait_ge(self.sem, self.base + self.n)

    def close(self):
        assert self.n == self.per, (self.n, self.per)


def spread(ap, n):
    return ap.unsqueeze(2).to_broadcast([ap.shape[0], ap.shape[1], n])


def repeat(ap, n):
    return ap.unsqueeze(1).to_broadcast([ap.shape[0], n, ap.shape[1]])


def constants(nc, keep, a):
    K = {}
    K["ident"] = keep.sb("ident", [P, P])
    K["tri"] = keep.sb("tri", [P, P])
    K["cap"] = keep.sb("cap", [P, P])
    K["ones"] = keep.sb("ones", [P, P])
    K["pc1"] = keep.sb("pc1", [P, PC1])
    K["pc2"] = keep.sb("pc2", [P, PC2])
    K["dtb"] = keep.sb("dtb", [P, SSM_H])
    K["alog"] = keep.sb("alog", [P, SSM_H])
    K["dskip"] = keep.sb("dskip", [P, SSM_H])
    K["gq"] = keep.sb("gq", [P, HD])
    K["gk"] = keep.sb("gk", [P, HD])
    K["sink"] = keep.sb("sink", [P, 2, KV_H])
    K["nsink"] = keep.sb("nsink", [P, 2, KV_H])
    K["sin"] = keep.sb("sin", [P, NT, RH])
    K["cos"] = keep.sb("cos", [P, NT, RH])
    with ExitStack() as ctx:
        r = Room(nc, ctx, "const")
        rows1, rows2 = r.sb("rows1", [PC1, P]), r.sb("rows2", [PC2, P])
        posi, posf = r.sb("posi", [NT, P], I32), r.sb("posf", [NT, P])
        pos = r.sb("pos", [P, NT])
        ang, turns = r.sb("ang", [P, NT, RH]), r.sb("turns", [P, 2, NT, RH])
        rest = r.sb("rest", [P, 2, NT, RH])
        psT = r.ps("psT", [P, HALF])
        loaded, made, filled = r.sem("loaded"), r.sem("made"), r.sem("filled")
        turned, columns = r.sem("turned"), r.sem("columns")
        pos_ready, angles, steps = r.sem("pos_ready"), r.sem("angles"), r.sem("steps")
        waves = r.sem("waves")
        loads = []

        def row_load(dst, src):
            loads.append((dst, src))

        row_load(rows1[PC_MIX:PC_MIX + NK, :], a["norm_mix"].rearrange("o (k p) -> (o k) p", p=P))
        row_load(rows1[PC_FFN:PC_FFN + NK, :], a["norm_ffn"].rearrange("o (k p) -> (o k) p", p=P))
        row_load(rows1[PC_SSM:PC_SSM + NK, :], a["ssm_norm"].rearrange("o (k p) -> (o k) p", p=P))
        row_load(rows1[PC_CW:PC_CB, :], a["conv_w"].rearrange("o j (k p) -> (o j k) p", p=P))
        row_load(rows1[PC_CB:PC1, :], a["conv_b"].rearrange("o (k p) -> (o k) p", p=P))
        row_load(rows2[0:PC_FB, :], a["ffn_conv_w"].rearrange("o j (k p) -> (o j k) p", p=P))
        row_load(rows2[PC_FB:PC2, :], a["ffn_conv_b"].rearrange("o (k p) -> (o k) p", p=P))
        row_load(posi[:, :], a["positions"].rearrange("o (t p) -> (o t) p", p=P))
        for name, src in (("dtb", "dt_bias"), ("alog", "a_log"), ("dskip", "d_skip"), ("gq", "q_norm"), ("gk", "k_norm")):
            row_load(K[name][:, :], a[src].to_broadcast([P, a[src].shape[1]]))
        by_row = a["sinks"].rearrange("o (j i c) -> o i c j", j=KV_H, i=2)
        for i in range(2):
            for c in range(2):
                row_load(K["sink"][i * CHUNK:(i + 1) * CHUNK, c, :], by_row[:, i, c, :].to_broadcast([CHUNK, KV_H]))

        with nc.Block() as block:

            @block.sync
            def _(sp):
                with nc.allow_non_contiguous_dma(reason="sixteen sinks"):
                    for dst, src in loads:
                        sp.dma_start(dst, src).then_inc(loaded, 16)

            @block.gpsimd
            def _(pool):
                nc.gpsimd.memset(K["ident"][:, :], 0.0).then_inc(filled, 1)
                nc.gpsimd.memset(K["tri"][:, :], 1.0).then_inc(filled, 1)
                nc.gpsimd.memset(K["cap"][:, :], BIG).then_inc(filled, 1)
                nc.gpsimd.memset(K["ones"][:, :], 1.0).then_inc(filled, 1)
                pool.wait_ge(filled, 4)
                nc.gpsimd.affine_select(out=K["ident"][:, :], in_=K["ident"][:, :], compare_op=ALU.not_equal, fill=1.0,
                                        base=0, pattern=[[-1, P]], channel_multiplier=1).then_inc(made, 1)
                for m, fill in (("tri", 0.0), ("cap", -BIG)):
                    nc.gpsimd.affine_select(out=K[m][:, :], in_=K[m][:, :], compare_op=ALU.is_ge, fill=fill,
                                            base=0, pattern=[[1, P]], channel_multiplier=-1).then_inc(made, 1)

            @block.tensor
            def _(pe):
                pe.wait_ge(loaded, 16 * len(loads))
                pe.wait_ge(made, 1)
                nc.tensor.transpose(psT[:, 0:PC1], rows1[:, :], K["ident"][0:PC1, 0:PC1]).then_inc(turned, 1)
                nc.tensor.transpose(psT[:, P:P + PC2], rows2[:, :], K["ident"][0:PC2, 0:PC2]).then_inc(turned, 1)
                pe.wait_ge(pos_ready, 1)
                nc.tensor.transpose(psT[:, 2 * P:2 * P + NT], posf[:, :], K["ident"][0:NT, 0:NT]).then_inc(turned, 1)

            @block.vector
            def _(dve):
                c = Chain(dve, steps)
                dve.wait_ge(loaded, 16 * len(loads))
                nc.vector.tensor_copy(posf[:, :], posi[:, :]).then_inc(pos_ready, 1)
                nc.vector.tensor_scalar(K["nsink"][:, :, :], K["sink"][:, :, :], -1.0, None, ALU.mult)
                dve.wait_ge(turned, 3)
                nc.vector.tensor_copy(K["pc1"][:, :], psT[:, 0:PC1]).then_inc(columns, 1)
                nc.vector.tensor_copy(K["pc2"][:, :], psT[:, P:P + PC2]).then_inc(columns, 1)
                c.link(nc.vector.tensor_copy(pos[:, :], psT[:, 2 * P:2 * P + NT]))
                inv_freq = np.float32(THETA) ** (-np.arange(0, ROPE, 2, dtype=np.float32) / np.float32(ROPE))
                for f in range(RH):
                    ins = nc.vector.tensor_scalar(ang[:, :, f], pos[:, :], float(inv_freq[f]), None, ALU.mult)
                c.link(ins)
                nearest = 1.5 * 2.0 ** 23
                for w, ahead in enumerate((0.0, 0.25)):
                    c.link(nc.vector.tensor_scalar(turns[:, w], ang[:, :, :], float(1 / (2 * np.pi)), ahead, ALU.mult, ALU.add))
                    c.link(nc.vector.tensor_scalar(turns[:, w], turns[:, w], nearest, None, ALU.add))
                    c.link(nc.vector.tensor_scalar(turns[:, w], turns[:, w], nearest, None, ALU.subtract))
                    left, src = 2 * np.pi, ang[:, :, :]
                    for part in range(4):
                        m, e = np.frexp(left)
                        piece = float(np.ldexp(np.floor(m * 256) / 256, e)) if part < 3 else float(np.float32(left))
                        left -= piece
                        c.link(nc.vector.scalar_tensor_tensor(rest[:, w], turns[:, w], -piece, src, ALU.mult, ALU.add))
                        src = rest[:, w]
                    if w:
                        c.link(nc.vector.tensor_scalar(rest[:, w], rest[:, w], float(np.pi / 2), None, ALU.add))
                    nc.vector.tensor_scalar(rest[:, w], rest[:, w], 3.1415925, -3.1415925, ALU.min, ALU.max).then_inc(angles, 1)

            @block.scalar
            def _(act):
                act.wait_ge(angles, 1)
                nc.scalar.activation(K["sin"][:, :, :], rest[:, 0], ACT.Sin).then_inc(waves, 1)
                act.wait_ge(angles, 2)
                nc.scalar.activation(K["cos"][:, :, :], rest[:, 1], ACT.Sin).then_inc(waves, 1)
        r.clear()
    return K


def norm_stage(nc, name, src, gain, K, x_sb, hT):
    with ExitStack() as ctx:
        r = Room(nc, ctx, name)
        junk = r.sb("junk", [P, D])
        ssq, rstd, power = r.sb("ssq", [P, NT]), r.sb("rstd", [P, NT]), r.sb("power", [P, 1])
        xn = r.sb("xn", [P, 2, D])
        full = r.sb("full", [P, 2, NK, P])
        psT = r.ps("psT", [P, 2, NK, P])
        x_in = [r.sem(f"x_in{t}") for t in range(NT)]
        squared, meaned, rstd_ready = r.sem("squared"), r.sem("meaned"), r.sem("rstd_ready")
        scaled, turned, gained = r.sem("scaled"), r.sem("turned"), r.sem("gained")
        hi_done, lo_done, set_power = r.sem("hi_done"), r.sem("lo_done"), r.sem("set_power")
        with nc.Block() as block:

            @block.sync
            def _(sp):
                for t in range(NT):
                    sp.dma_start(x_sb[:, t, :], src[t * P:(t + 1) * P, :]).then_inc(x_in[t], 16)

            @block.scalar
            def _(act):
                def square(t):
                    act.wait_ge(x_in[t], 16)
                    if t:
                        act.wait_ge(squared, t)
                    nc.scalar.activation(junk[:, :], x_sb[:, t, :], ACT.Square, accum_out=ssq[:, t:t + 1]).then_inc(squared, 1)

                square(0)
                for t in range(NT):
                    if t + 1 < NT:
                        square(t + 1)
                    act.wait_ge(gained, t + 1)
                    nc.scalar.activation(hT["hi"][:, :, t * P:(t + 1) * P], full[:, t % 2], ACT.Copy).then_inc(hi_done, 1)

            @block.gpsimd
            def _(pool):
                nc.gpsimd.memset(power[:, :], -0.5).then_inc(set_power, 1)
                pool.wait_ge(set_power, 1)
                for t in range(NT):
                    one = slice(t, t + 1)
                    pool.wait_ge(squared, t + 1)
                    nc.gpsimd.tensor_scalar(rstd[:, one], ssq[:, one], 1.0 / D, EPS, ALU.mult, ALU.add).then_inc(meaned, 1)
                    pool.wait_ge(meaned, t + 1)
                    nc.gpsimd.tensor_tensor(rstd[:, one], rstd[:, one], power[:, :], ALU.pow).then_inc(rstd_ready, 1)

            @block.vector
            def _(dve):
                def scale(t):
                    dve.wait_ge(rstd_ready, t + 1)
                    if t >= 2:
                        dve.wait_ge(turned, t - 1)
                    nc.vector.tensor_scalar(xn[:, t % 2], x_sb[:, t, :], rstd[:, t:t + 1], None, ALU.mult).then_inc(scaled, 1)

                scale(0)
                for t in range(NT):
                    if t + 1 < NT:
                        scale(t + 1)
                    dve.wait_ge(turned, t + 1)
                    if t >= 2:
                        dve.wait_ge(hi_done, t - 1)
                        dve.wait_ge(lo_done, t - 1)
                    nc.vector.tensor_tensor(full[:, t % 2], psT[:, t % 2], spread(K["pc1"][:, gain:gain + NK], P), ALU.mult).then_inc(gained, 1)
                    dve.wait_ge(gained, t + 1)
                    dve.wait_ge(hi_done, t + 1)
                    nc.vector.tensor_tensor(hT["lo"][:, :, t * P:(t + 1) * P], full[:, t % 2],
                                            hT["hi"][:, :, t * P:(t + 1) * P].bitcast(F32), ALU.subtract).then_inc(lo_done, 1)

            @block.tensor
            def _(pe):
                for t in range(NT):
                    pe.wait_ge(scaled, t + 1)
                    if t >= 2:
                        pe.wait_ge(gained, t - 1)
                    for k in range(NK):
                        ins = nc.tensor.transpose(psT[:, t % 2, k, :], xn[:, t % 2, k * P:(k + 1) * P], K["ident"][:, :])
                    ins.then_inc(turned, 1)
        r.clear()


def product(nc, out, w, h, first, last):
    for n, (a, b) in enumerate(PASSES):
        ins = nc.tensor.matmul(out, w[a], h[b], start=first and n == 0, stop=last and n == len(PASSES) - 1)
    return ins


def xbc_stage(nc, a, K, hT, xbcT, S):
    w_in = a["w_in"].rearrange("o (k p) c -> p (o k) c", p=P)
    with ExitStack() as ctx:
        r = Room(nc, ctx, "xbc")
        raw = r.sb("raw", [P, 2, NK, P])
        w = {part: r.sb(f"w_{part}", [P, 2, NK, P], F32R) for part in ("hi", "lo")}
        wdt_raw = r.sb("wdt_raw", [P, NK, SSM_H])
        wdt = {part: r.sb(f"wdt_{part}", [P, NK, SSM_H], F32R) for part in ("hi", "lo")}
        pre = r.sb("pre", [P, SSM_CONV - 1 + L])
        conv = r.sb("conv", [P, L])
        act_out = r.sb("act_out", [P, 2, L])
        ps = r.ps("ps", [P, 2, 2, HALF])
        ps_dt = r.ps("ps_dt", [P, NT, SSM_H])
        ps_sum = r.ps("ps_sum", [P, 2, NT * SSM_H])
        t1, t2, t3, t4 = (r.sb(f"t{n}", [P, NT, SSM_H]) for n in range(4))
        ea = r.sb("ea", [P, SSM_H])
        raw_in = [r.sem(f"raw_in{u}") for u in range(2)]
        stored = [r.sem(f"stored{u}") for u in range(2)]
        dt_in, dt_hi, dt_lo = r.sem("dt_in"), r.sem("dt_hi"), r.sem("dt_lo")
        w_hi, w_lo, mm, evac = r.sem("w_hi"), r.sem("w_lo"), r.sem("mm"), r.sem("evac")
        padded, conv_step, conv_done, silu = r.sem("padded"), r.sem("conv_step"), r.sem("conv_done"), r.sem("silu")
        dt_mm, dve_dt, act_dt, da_ready, sums = r.sem("dt_mm"), r.sem("dve_dt"), r.sem("act_dt"), r.sem("da_ready"), r.sem("sums")
        NP_ = NB_XBC // 2

        def turns(eng, body):
            body(0, True, False)
            with eng.Fori(1, NP_ - 1) as i:
                body(i, False, False)
            body(NP_ - 1, False, True)

        with nc.Block() as block:

            @block.sync
            def _(sp):
                sp.dma_start(wdt_raw[:, :, :], w_in[:, :, DT0:DT0 + SSM_H]).then_inc(dt_in, 16)

                def body(i, first, last):
                    for u in range(2):
                        b = i * 2 + u
                        if not first:
                            sp.wait_ge(w_hi, b - 1)
                            sp.wait_ge(w_lo, b - 1)
                        sp.dma_start(raw[:, u], w_in[:, :, ds(b * P + XBC0, P)]).then_inc(raw_in[u], 16)

                turns(sp, body)

            @block.scalar
            def _(act):
                def split(i, u, early):
                    b = i * 2 + u
                    act.wait_ge(raw_in[u], i * 16 + 16)
                    if not early:
                        act.wait_ge(mm, b - 1)
                    nc.scalar.activation(w["hi"][:, u], raw[:, u], ACT.Copy).then_inc(w_hi, 1)

                def body(i, first, last):
                    for u in range(2):
                        b = i * 2 + u
                        if u == 0:
                            split(i, 1, first)
                        elif not last:
                            split(i + 1, 0, False)
                        act.wait_ge(mm, b + 1)
                        if not (first and u == 0):
                            act.wait_ge(conv_done, b)
                        else:
                            act.wait_ge(padded, 1)
                        nc.scalar.activation(pre[:, SSM_CONV - 1:], ps[:, u].rearrange("p a b -> p (a b)"), ACT.Copy).then_inc(evac, 1)
                        act.wait_ge(conv_done, b + 1)
                        if not first:
                            act.wait_ge(stored[u], i * 16)
                        nc.scalar.activation(act_out[:, u], conv[:, :], ACT.Silu).then_inc(silu, 1)
                        act.wait_ge(silu, b + 1)
                        act.dma_start(xbcT[ds(b * P, P), :], act_out[:, u]).then_inc(stored[u], 16)

                act.wait_ge(dt_in, 16)
                nc.scalar.activation(wdt["hi"][:, :, :], wdt_raw[:, :, :], ACT.Copy).then_inc(dt_hi, 1)
                split(0, 0, True)
                turns(act, body)
                nc.scalar.activation(ea[:, :], K["alog"][:, :], ACT.Exp).then_inc(act_dt, 1)
                act.wait_ge(dve_dt, 2)
                nc.scalar.activation(t2[:, :, :], t2[:, :, :], ACT.Exp, scale=-1.0).then_inc(act_dt, 1)
                act.wait_ge(dve_dt, 3)
                nc.scalar.activation(t4[:, :, :], t3[:, :, :], ACT.Ln).then_inc(act_dt, 1)
                act.wait_ge(dve_dt, 15)
                nc.scalar.activation(S["eacs"][:, :, :], t1[:, :, :], ACT.Exp).then_inc(act_dt, 1)
                nc.scalar.activation(S["cdec"][:, :, :], ps_sum[:, 1].rearrange("p (t h) -> p t h", h=SSM_H), ACT.Exp).then_inc(act_dt, 1)
                nc.scalar.activation(t2[:, :, :], t2[:, :, :], ACT.Exp).then_inc(act_dt, 1)
                for u in range(2):
                    act.wait_ge(stored[u], 16 * NP_)

            @block.vector
            def _(dve):
                c = Chain(dve, conv_step, 2 * SSM_CONV - 2)

                def split(i, u, early):
                    b = i * 2 + u
                    if not early:
                        dve.wait_ge(mm, b - 1)
                    dve.wait_ge(w_hi, b + 1)
                    nc.vector.tensor_tensor(w["lo"][:, u], raw[:, u], w["hi"][:, u].bitcast(F32), ALU.subtract).then_inc(w_lo, 1)

                def body(i, first, last):
                    c.turn(i)
                    for u in range(2):
                        b = i * 2 + u
                        if u == 0:
                            split(i, 1, first)
                        elif not last:
                            split(i + 1, 0, False)
                        tap = lambda j: K["pc1"][:, ds(b + PC_CW + j * NB_XBC, 1)]
                        dve.wait_ge(evac, b + 1)
                        if not (first and u == 0):
                            dve.wait_ge(silu, b)
                        c.link(nc.vector.tensor_scalar(conv[:, :], pre[:, SSM_CONV - 1:], tap(SSM_CONV - 1), K["pc1"][:, ds(b + PC_CB, 1)], ALU.mult, ALU.add))
                        for j in range(SSM_CONV - 2, -1, -1):
                            ins = nc.vector.scalar_tensor_tensor(conv[:, :], pre[:, j:j + L], tap(j), conv[:, :], ALU.mult, ALU.add)
                            if j:
                                c.link(ins)
                            else:
                                ins.then_inc(conv_done, 1)
                    c.close()

                nc.vector.memset(pre[:, 0:SSM_CONV - 1], 0.0).then_inc(padded, 1)
                dve.wait_ge(dt_hi, 1)
                nc.vector.tensor_tensor(wdt["lo"][:, :, :], wdt_raw[:, :, :], wdt["hi"][:, :, :].bitcast(F32), ALU.subtract).then_inc(dt_lo, 1)
                split(0, 0, True)
                turns(dve, body)
                d = Chain(dve, dve_dt)
                dve.wait_ge(dt_mm, 1)
                d.link(nc.vector.tensor_tensor(t1[:, :, :], ps_dt[:, :, :], repeat(K["dtb"][:, :], NT), ALU.add))
                d.link(nc.vector.scalar_tensor_tensor(t2[:, :, :], t1[:, :, :], -1.0, t1[:, :, :], ALU.mult, ALU.max))
                dve.wait_ge(act_dt, 2)
                d.link(nc.vector.tensor_scalar(t3[:, :, :], t2[:, :, :], 1.0, None, ALU.add))
                dve.wait_ge(act_dt, 3)
                d.link(nc.vector.tensor_scalar(t3[:, :, :], t3[:, :, :], 1.0, None, ALU.subtract))
                d.link(nc.vector.tensor_scalar(S["dt"][:, :, :], t3[:, :, :], 0.0, None, ALU.is_equal))
                d.link(nc.vector.tensor_tensor(t3[:, :, :], t3[:, :, :], S["dt"][:, :, :], ALU.add))
                d.link(nc.vector.tensor_tensor(t4[:, :, :], t4[:, :, :], S["dt"][:, :, :], ALU.add))
                d.link(nc.vector.reciprocal(t3[:, :, :], t3[:, :, :]))
                d.link(nc.vector.tensor_tensor(t4[:, :, :], t4[:, :, :], t3[:, :, :], ALU.mult))
                d.link(nc.vector.tensor_tensor(t4[:, :, :], t4[:, :, :], t2[:, :, :], ALU.mult))
                d.link(nc.vector.scalar_tensor_tensor(S["dt"][:, :, :], t1[:, :, :], 0.0, t4[:, :, :], ALU.max, ALU.add))
                d.link(nc.vector.tensor_tensor(t1[:, :, :], S["dt"][:, :, :], repeat(ea[:, :], NT), ALU.mult))
                nc.vector.tensor_scalar(S["dA"][:, :, :], t1[:, :, :], -1.0, None, ALU.mult).then_inc(da_ready, 1)
                dve.wait_ge(sums, 1)
                acs = ps_sum[:, 0].rearrange("p (t h) -> p t h", h=SSM_H)
                tot = ps_sum[:, 1].rearrange("p (t h) -> p t h", h=SSM_H)
                d.link(nc.vector.tensor_copy(t1[:, :, :], acs))
                nc.vector.tensor_scalar(S["nacs"][:, :, :], t1[:, :, :], -1.0, None, ALU.mult)
                d.link(nc.vector.tensor_tensor(t2[:, :, :], tot, t1[:, :, :], ALU.subtract))
                d.link(nc.vector.memset(t3[:, 0, 0:1], 0.0))
                dve.wait_ge(act_dt, 6)
                d.link(nc.vector.tensor_tensor(S["wend"][:, :, :], t2[:, :, :], S["dt"][:, :, :], ALU.mult))

            @block.tensor
            def _(pe):
                def body(i, first, last):
                    for u in range(2):
                        b = i * 2 + u
                        pe.wait_ge(w_lo, b + 1)
                        if not first:
                            pe.wait_ge(evac, b - 1)
                        for half in range(2):
                            for k in range(NK):
                                ins = product(nc, ps[:, u, half], {p: w[p][:, u, k, :] for p in w},
                                              {p: hT[p][:, k, half * HALF:(half + 1) * HALF] for p in w}, k == 0, k == NK - 1)
                        ins.then_inc(mm, 1)

                pe.wait_ge(dt_lo, 1)
                for t in range(NT):
                    for k in range(NK):
                        ins = product(nc, ps_dt[:, t, :], {p: hT[p][:, k, t * P:(t + 1) * P] for p in w},
                                      {p: wdt[p][:, k, :] for p in w}, k == 0, k == NK - 1)
                ins.then_inc(dt_mm, 1)
                turns(pe, body)
                pe.wait_ge(da_ready, 1)
                dA = S["dA"][:, :, :].rearrange("p t h -> p (t h)")
                nc.tensor.matmul(ps_sum[:, 0], K["tri"][:, :], dA, start=True, stop=True)
                nc.tensor.matmul(ps_sum[:, 1], K["ones"][:, :], dA, start=True, stop=True).then_inc(sums, 1)
        r.clear()


def scan_stage(nc, a, K, hT, xbcT, S, proj, y_out):
    w_in = a["w_in"].rearrange("o (k p) c -> p (o k) c", p=P)
    proj_v = proj.rearrange("(t p) c -> p t c", p=P)
    xbc_v = xbcT.rearrange("(b p) l -> p b l", p=P)
    NX = SSM_W // P
    HS = 4
    NS = SSM_H // HS
    with ExitStack() as ctx:
        r = Room(nc, ctx, "scan")
        raw = r.sb("raw", [P, NK, PB])
        w = {part: r.sb(f"w_{part}", [P, 2, NK, PB], F32R) for part in ("hi", "lo")}
        stage = r.sb("stage", [P, 2, NT, PB])
        xc = r.sb("xc", [P, 2, NB_XBC, P])
        spread_dA = r.sb("spread_dA", [P, NS, HS, P])
        W = r.sb("W", [P, SSM_H, P])
        xt, xdt, xw, xd = (r.sb(n, [P, SSM_H, SSM_P]) for n in ("xt", "xdt", "xw", "xd"))
        bt = r.sb("bt", [P, SSM_G, P])
        off = r.sb("off", [P, SSM_H, SSM_P])
        y = r.sb("y", [P, 2, SSM_H, SSM_P])
        state = r.sb("state", [P, SSM_H, SSM_P])
        ps = r.ps("ps", [P, 2, 2, PB])
        ps_x = r.ps("ps_x", [P, SSM_H, SSM_P])
        ps_bc = r.ps("ps_bc", [P, 2, SSM_G, P])
        ps_s = r.ps("ps_s", [P, HS, P])
        ps_y = r.ps("ps_y", [P, SSM_H, SSM_P])
        raw_in, w_hi, w_lo = r.sem("raw_in"), r.sem("w_hi"), r.sem("w_lo")
        unit_mm, unit_evac = r.sem("unit_mm"), r.sem("unit_evac")
        stored = [r.sem(f"stored{u}") for u in range(2)]
        y_stored = [r.sem(f"y_stored{u}") for u in range(2)]
        xc_in = [r.sem(f"xc_in{u}") for u in range(2)]
        x_turned, bc_mm, x_copied, bt_copied = r.sem("x_turned"), r.sem("bc_mm"), r.sem("x_copied"), r.sem("bt_copied")
        dA_spread, decay_mm, seg_done, exp_done = r.sem("dA_spread"), r.sem("decay_mm"), r.sem("seg_done"), r.sem("exp_done")
        W_done, xdt_done, xw_done, xd_done = r.sem("W_done"), r.sem("xdt_done"), r.sem("xw_done"), r.sem("xd_done")
        off_mm, off_scaled, off_skip = r.sem("off_mm"), r.sem("off_scaled"), r.sem("off_skip")
        y_mm, y_done, state_mm, state_faded, state_done = r.sem("y_mm"), r.sem("y_done"), r.sem("state_mm"), r.sem("state_faded"), r.sem("state_done")
        decays = [ps_s[:, :, :], ps_y[:, 0:HPG, :].rearrange("p (h c) q -> p h (c q)", c=2),
                  ps_y[:, HPG:, :].rearrange("p (h c) q -> p h (c q)", c=2), ps_s[:, :, :]]
        NJ = NT // 2
        NU = NT // 2
        kv_at = lambda n: KV0 + n * PB

        def scalars(name, t, n=SSM_P):
            return S[name][:, ds(t, 1), :].rearrange("p o h -> p (o h)").unsqueeze(2).to_broadcast([P, SSM_H, n])

        def turns(eng, body):
            body(0, True)
            with eng.Fori(1, NJ) as j:
                body(j, False)

        with nc.Block() as block:

            @block.sync
            def _(sp):
                def weights(n, first, col):
                    if not first:
                        sp.wait_ge(w_hi, n)
                        sp.wait_ge(w_lo, n)
                    sp.dma_start(raw[:, :, :], w_in[:, :, ds(col, PB)]).then_inc(raw_in, 16)

                def tile(j, u, first):
                    if not first:
                        sp.wait_ge(off_mm, j * 2 + u - 1)
                    sp.dma_start(xc[:, u], xbc_v[:, :, ds((j * 2 + u) * P, P)]).then_inc(xc_in[u], 16)

                def body(j, first):
                    tile(j, 0, first)
                    weights(j * 2 + 2, False, j * PB + Z0)
                    tile(j, 1, first)
                    weights(j * 2 + 3, False, j * PB + Q0)

                weights(0, True, kv_at(0))
                weights(1, False, kv_at(1))
                turns(sp, body)

            @block.scalar
            def _(act):
                def split(n, u, first=False):
                    act.wait_ge(raw_in, n * 16 + 16)
                    if not first:
                        act.wait_ge(unit_mm, (n - 1) * NU)
                    nc.scalar.activation(w["hi"][:, u], raw[:, :, :], ACT.Copy).then_inc(w_hi, 1)

                def evacuate(n, u, func, col, stored_before):
                    if stored_before is not None:
                        act.wait_ge(stored[u], stored_before)
                    for m in range(NU):
                        act.wait_ge(unit_mm, n * NU + m + 1)
                        nc.scalar.activation(stage[:, u, 2 * m:2 * m + 2, :], ps[:, m % 2], func).then_inc(unit_evac, 1)
                    act.wait_ge(unit_evac, n * NU + NU)
                    act.dma_start(proj_v[:, :, ds(col, PB)], stage[:, u]).then_inc(stored[u], 16)

                def tile(t, first):
                    act.wait_ge(x_turned, t + 1)
                    if not first:
                        act.wait_ge(xd_done, t)
                    nc.scalar.activation(xt[:, :, :], ps_x[:, :, :], ACT.Copy).then_inc(x_copied, 1)
                    act.wait_ge(bc_mm, t + 1)
                    if not first:
                        act.wait_ge(state_mm, t)
                    nc.scalar.activation(bt[:, :, :], ps_bc[:, 0], ACT.Copy).then_inc(bt_copied, 1)
                    for s in range(NS):
                        act.wait_ge(seg_done, t * NS + s + 1)
                        grp = W[:, HS * s:HS * (s + 1), :]
                        nc.scalar.activation(grp, grp, ACT.Exp).then_inc(exp_done, 1)

                def body(j, first, last):
                    tile(j * 2, first)
                    split(j * 2 + 3, 1)
                    evacuate(j * 2 + 2, 0, ACT.Silu, j * PB, j * 16 + 16)
                    tile(j * 2 + 1, False)
                    if not last:
                        split(j * 2 + 4, 0)
                    evacuate(j * 2 + 3, 1, ACT.Copy, j * PB + SSM_W, j * 16 + 16)

                split(0, 0, True)
                split(1, 1, True)
                evacuate(0, 0, ACT.Copy, SSM_W + Q_H * HD, None)
                split(2, 0)
                evacuate(1, 1, ACT.Copy, SSM_W + Q_H * HD + PB, None)
                body(0, True, False)
                with act.Fori(1, NJ - 1) as j:
                    body(j, False, False)
                body(NJ - 1, False, True)
                for u in range(2):
                    act.wait_ge(stored[u], 16 * (NJ + 1))

            @block.gpsimd
            def _(pool):
                def tile(t, u, first):
                    for s in range(NS):
                        if not first:
                            pool.wait_ge(decay_mm, t * NS - (NS - 1 - s))
                        heads = S["dA"][:, ds(t, 1), HS * s:HS * (s + 1)].rearrange("p o h -> p (o h)")
                        nc.gpsimd.tensor_tensor(spread_dA[:, s], repeat(K["tri"][:, :], HS), spread(heads, P), ALU.mult).then_inc(dA_spread, 1)
                    pool.wait_ge(x_copied, t + 1)
                    if not first:
                        pool.wait_ge(y_mm, t)
                        pool.wait_ge(state_mm, t)
                        pool.wait_ge(off_skip, t)
                    nc.gpsimd.tensor_tensor(xdt[:, :, :], xt[:, :, :], scalars("dt", t), ALU.mult).then_inc(xdt_done, 1)
                    nc.gpsimd.tensor_tensor(xw[:, :, :], xt[:, :, :], scalars("wend", t), ALU.mult).then_inc(xw_done, 1)
                    nc.gpsimd.tensor_tensor(xd[:, :, :], xt[:, :, :], spread(K["dskip"][:, :], SSM_P), ALU.mult).then_inc(xd_done, 1)
                    pool.wait_ge(xd_done, t + 1)
                    pool.wait_ge(off_scaled, t + 1)
                    nc.gpsimd.tensor_tensor(off[:, :, :], off[:, :, :], xd[:, :, :], ALU.add).then_inc(off_skip, 1)
                    pool.wait_ge(y_done, t + 1)
                    pool.dma_start(y_out[ds(t * P, P), :], y[:, u].rearrange("p h q -> p (h q)")).then_inc(y_stored[u], 16)

                def body(j, first):
                    for u in range(2):
                        tile(j * 2 + u, u, first and u == 0)

                turns(pool, body)
                for u in range(2):
                    pool.wait_ge(y_stored[u], 16 * NJ)

            @block.vector
            def _(dve):
                def split(n, u, first=False):
                    dve.wait_ge(w_hi, n + 1)
                    if not first:
                        dve.wait_ge(unit_mm, (n - 1) * NU)
                    nc.vector.tensor_tensor(w["lo"][:, u], raw[:, :, :], w["hi"][:, u].bitcast(F32), ALU.subtract).then_inc(w_lo, 1)

                def before(t, first):
                    for s in range(NS):
                        dve.wait_ge(decay_mm, t * NS + s + 1)
                        if not first and s == 0:
                            dve.wait_ge(y_mm, t)
                        for h in range(HS):
                            head = HS * s + h
                            ins = nc.vector.scalar_tensor_tensor(W[:, head, :], decays[s][:, h, :], S["nacs"][:, ds(t, 1), head],
                                                                 K["cap"][:, :], ALU.add, ALU.min)
                        ins.then_inc(seg_done, 1)
                    for g in range(SSM_G):
                        dve.wait_ge(exp_done, t * NS + (g + 1) * NS // SSM_G)
                        heads = W[:, HPG * g:HPG * (g + 1), :]
                        nc.vector.tensor_tensor(heads, heads, repeat(ps_bc[:, 1, g, :], HPG), ALU.mult).then_inc(W_done, 1)

                def after(t, u, first, y_before):
                    dve.wait_ge(off_mm, t + 1)
                    if not first:
                        dve.wait_ge(y_done, t)
                    nc.vector.tensor_tensor(off[:, :, :], ps_x[:, :, :], scalars("eacs", t), ALU.mult).then_inc(off_scaled, 1)
                    if not first:
                        dve.wait_ge(state_done, t)
                    nc.vector.tensor_tensor(state[:, :, :], state[:, :, :], scalars("cdec", t), ALU.mult).then_inc(state_faded, 1)
                    dve.wait_ge(y_mm, t + 1)
                    dve.wait_ge(off_skip, t + 1)
                    if y_before is not None:
                        dve.wait_ge(y_stored[u], y_before)
                    nc.vector.tensor_tensor(y[:, u], ps_y[:, :, :], off[:, :, :], ALU.add).then_inc(y_done, 1)
                    dve.wait_ge(state_mm, t + 1)
                    dve.wait_ge(state_faded, t + 2)
                    nc.vector.tensor_tensor(state[:, :, :], ps_x[:, :, :], state[:, :, :], ALU.add).then_inc(state_done, 1)

                def body(j, first, last):
                    for u in range(2):
                        t = j * 2 + u
                        before(t, first and u == 0)
                        if not (last and u == 1):
                            split(j * 2 + 3 + u, 1 - u)
                        after(t, u, first and u == 0, None if first else j * 16)

                nc.vector.memset(state[:, :, :], 0.0).then_inc(state_faded, 1)
                split(0, 0, True)
                split(1, 1, True)
                split(2, 0)
                dve.wait_ge(state_faded, 1)
                body(0, True, False)
                with dve.Fori(1, NJ - 1) as j:
                    body(j, False, False)
                body(NJ - 1, False, True)

            @block.tensor
            def _(pe):
                def project(n, u, first=False):
                    pe.wait_ge(w_lo, n + 1)
                    for t in range(NT):
                        m = t // 2
                        if t % 2 == 0 and not (first and m < 2):
                            pe.wait_ge(unit_evac, n * NU + m - 1)
                        for k in range(NK):
                            ins = product(nc, ps[:, m % 2, t % 2, :], {p: hT[p][:, k, t * P:(t + 1) * P] for p in w},
                                          {p: w[p][:, u, k, :] for p in w}, k == 0, k == NK - 1)
                        if t % 2:
                            ins.then_inc(unit_mm, 1)

                def before(t, u, first, xc_full):
                    pe.wait_ge(xc_in[u], xc_full)
                    if not first:
                        pe.wait_ge(state_done, t)
                    for b in range(NX):
                        ins = nc.tensor.transpose(ps_x[:, 2 * b:2 * b + 2, :].rearrange("p a b -> p (a b)"), xc[:, u, b, :], K["ident"][:, :])
                    ins.then_inc(x_turned, 1)
                    if not first:
                        pe.wait_ge(W_done, t * SSM_G)
                    for g in range(SSM_G):
                        nc.tensor.transpose(ps_bc[:, 0, g, :], xc[:, u, NX + g, :], K["ident"][:, :])
                        ins = nc.tensor.matmul(ps_bc[:, 1, g, :], xc[:, u, NX + g, :], xc[:, u, NX + SSM_G + g, :], start=True, stop=True)
                    ins.then_inc(bc_mm, 1)
                    for s in range(NS):
                        pe.wait_ge(dA_spread, t * NS + s + 1)
                        if s == 0 and not first:
                            pe.wait_ge(seg_done, t * NS)
                        if s == 1 and not first:
                            pe.wait_ge(y_done, t)
                        if s == 3:
                            pe.wait_ge(seg_done, t * NS + 1)
                        nc.tensor.matmul(decays[s], K["ones"][:, :], spread_dA[:, s], start=True, stop=True).then_inc(decay_mm, 1)

                def after(t, u, first):
                    pe.wait_ge(x_copied, t + 1)
                    if not first:
                        pe.wait_ge(state_done, t)
                    for g in range(SSM_G):
                        ins = nc.tensor.matmul(ps_x[:, HPG * g:HPG * (g + 1), :], xc[:, u, NX + SSM_G + g, :], state[:, HPG * g:HPG * (g + 1), :],
                                               start=True, stop=True)
                    ins.then_inc(off_mm, 1)
                    pe.wait_ge(xdt_done, t + 1)
                    pe.wait_ge(seg_done, t * NS + 3)
                    for h in range(SSM_H):
                        if h % HPG == 0:
                            pe.wait_ge(W_done, t * SSM_G + h // HPG + 1)
                        ins = nc.tensor.matmul(ps_y[:, h, :], W[:, h, :], xdt[:, h, :], start=True, stop=True)
                    ins.then_inc(y_mm, 1)
                    pe.wait_ge(bt_copied, t + 1)
                    pe.wait_ge(xw_done, t + 1)
                    pe.wait_ge(off_scaled, t + 1)
                    for g in range(SSM_G):
                        ins = nc.tensor.matmul(ps_x[:, HPG * g:HPG * (g + 1), :], bt[:, g, :], xw[:, HPG * g:HPG * (g + 1), :], start=True, stop=True)
                    ins.then_inc(state_mm, 1)

                def body(j, first):
                    for u in range(2):
                        t = j * 2 + u
                        before(t, u, first and u == 0, j * 16 + 16)
                        project(j * 2 + 2 + u, u)
                        after(t, u, first and u == 0)

                project(0, 0, True)
                project(1, 1)
                pe.wait_ge(state_faded, 1)
                turns(pe, body)
        r.clear()


def mix_stage(nc, a, K, proj, y_in, x_new):
    w_out = a["w_out"].rearrange("o (m p) c -> p (o m) c", p=P)
    x = a["x"].rearrange("o t d -> (o t) d")
    NQB = Q_H * HD // P
    QW, QKW = Q_H * HD, QK_H * HD
    ROWS = 2 * KV_H
    NW = 8
    WB = NM * 2 // NW
    with ExitStack() as ctx:
        r = Room(nc, ctx, "mix")
        with nc.sbuf_tensor("mix_w_raw", [P, NM, D], F32) as w_raw:
            pass
        w = {part: r.sb(f"w_{part}", [P, NM, D], F32R) for part in ("lo", "hi")}
        mix = {part: r.sb(f"mix_{part}", [P, NM, P], F32R) for part in ("hi", "lo")}
        qk, qn = r.sb("qk", [P, QK_H, HD]), r.sb("qn", [P, QK_H, HD])
        v_own, v_mixed = r.sb("v_own", [P, KV_W]), r.sb("v_mixed", [P, KV_W])
        yz, x_io = r.sb("yz", [P, 2, D]), r.sb("x_io", [P, D])
        kd = r.sb("kd", [P, KV_H, 2, HD])
        qT = r.sb("qT", [P, 2, NQB, CHUNK])
        kT = r.sb("kT", [P, KV_H, 3, CHUNK])
        prob, probT = r.sb("prob", [P, 2, ROWS, P]), r.sb("probT", [P, 2, ROWS, P])
        full = r.sb("full", [P, NK, P])
        rope = r.sb("rope", [P, 4, QK_H, RH])
        qk_ms, qk_rs = r.sb("qk_ms", [P, QK_H]), r.sb("qk_rs", [P, QK_H])
        y_ms, y_rs = r.sb("y_ms", [P, 1]), r.sb("y_rs", [P, 1])
        power, eps = r.sb("power", [P, QK_H]), r.sb("eps", [P, QK_H])
        top, ntop, sink_arg = (r.sb(n, [P, 2, ROWS]) for n in ("top", "ntop", "sink_arg"))
        sink_exp, row_sum, inv = (r.sb(n, [P, 2, ROWS]) for n in ("sink_exp", "row_sum", "inv"))
        ps_s = r.ps("ps_s", [P, ROWS, P])
        ps_t = r.ps("ps_t", [P, ROWS, P])
        ps_a = r.ps("ps_a", [P, NQB, 2, CHUNK])
        ps_o = r.ps("ps_o", [P, 2, HALF])
        w_in = [r.sem(f"w_in{n}") for n in range(NW)]
        w_hi, w_lo = r.sem("w_hi"), r.sem("w_lo")
        qk_in, z_in, y_in_, x_in = r.sem("qk_in"), r.sem("z_in"), r.sem("y_in"), r.sem("x_in")
        v_own_in, v_own2_in, v_before_in = r.sem("v_own_in"), r.sem("v_own2_in"), r.sem("v_before_in")
        x_out = r.sem("x_out")
        set_power = r.sem("set_power")
        qk_squared, qk_summed, qk_eps, qk_rs_ready = r.sem("qk_squared"), r.sem("qk_summed"), r.sem("qk_eps"), r.sem("qk_rs_ready")
        qk_step, qk_read, qn_done, kd_done = r.sem("qk_step"), r.sem("qk_read"), r.sem("qn_done"), r.sem("kd_done")
        q_turned, k_turned, qT_done, kT_moved, kT_done = (r.sem(n) for n in ("q_turned", "k_turned", "qT_done", "kT_moved", "kT_done"))
        s_mm, top_step, ntop_done, exp_done = r.sem("s_mm"), r.sem("top_step"), r.sem("ntop_done"), r.sem("exp_done")
        inv_step, prob_done, prob_turned, probT_done, pv_mm = (r.sem(n) for n in ("inv_step", "prob_done", "prob_turned", "probT_done", "pv_mm"))
        at_hi, at_lo = r.sem("at_hi"), r.sem("at_lo")
        gated, y_squared, y_eps, y_rs_ready, y_scaled = (r.sem(n) for n in ("gated", "y_squared", "y_eps", "y_rs_ready", "y_scaled"))
        y_turned, gained, y_hi, y_lo = (r.sem(n) for n in ("y_turned", "gained", "y_hi", "y_lo"))
        out_mm, out_added = r.sem("out_mm"), r.sem("out_added")
        yt, zt = yz[:, 0], yz[:, 1]

        def piece(n):
            half, part = n // (NW // 2), n // (NW // 4) % 2
            row = (1 - part) * NK + n % (NW // 4) * WB
            return slice(row, row + WB), slice(half * HALF, (half + 1) * HALF)

        w_part = lambda which, n: w[which][:, piece(n)[0], piece(n)[1]]
        w_raw_part = lambda n: w_raw[:, piece(n)[0], piece(n)[1]]
        w_out_part = lambda n: w_out[:, piece(n)[0], piece(n)[1]]
        flat = lambda ap: ap.rearrange("p a b -> p (a b)")

        def tiles(eng, body):
            body(0, True, False)
            with eng.Fori(1, NT - 1) as t:
                body(t, False, False)
            body(NT - 1, False, True)

        with nc.Block() as block:

            @block.sync
            def _(sp):
                qk_cols = slice(SSM_W, SSM_W + QKW)
                v_cols = slice(SSM_W + QKW, SSM_W + QKW + KV_W)

                def load_qk(t):
                    sp.dma_start(qk[:, :, :], proj[ds(t * P, P), qk_cols].rearrange("t (h d) -> t h d", d=HD)).then_inc(qk_in, 16)

                def load_yz(t):
                    sp.dma_start(yt, y_in[ds(t * P, P), :]).then_inc(y_in_, 16)
                    sp.dma_start(zt, proj[ds(t * P, P), 0:SSM_W]).then_inc(z_in, 16)

                def store(t):
                    sp.wait_ge(out_added, t * 2 + 2)
                    sp.dma_start(x_new[ds(t * P, P), :], x_io[:, :]).then_inc(x_out, 16)
                    sp.wait_ge(x_out, t * 16 + 16)

                def body(t, stores, loads_qk, loads):
                    if stores:
                        store(t - 2)
                        sp.dma_start(x_io[:, :], x[ds((t - 1) * P, P), :]).then_inc(x_in, 16)
                    if loads:
                        sp.wait_ge(y_turned, t + 1)
                        load_yz(t + 1)
                    if loads_qk:
                        sp.wait_ge(qk_read, t + 2)
                        load_qk(t + 2)
                    if loads:
                        sp.wait_ge(pv_mm, t * 2 + 2)
                        sp.dma_start(v_own[:, :], proj[ds(t * P + P, P), v_cols]).then_inc(v_own_in, 16)
                        sp.dma_start(v_mixed[0:CHUNK, :], proj[ds(t * P + P, CHUNK), v_cols]).then_inc(v_own2_in, 16)
                        sp.dma_start(v_mixed[CHUNK:, :], proj[ds(t * P + CHUNK, CHUNK), v_cols]).then_inc(v_before_in, 16)

                load_qk(0)
                load_yz(0)
                sp.dma_start(v_own[:, :], proj[0:P, v_cols]).then_inc(v_own_in, 16)
                sp.dma_start(v_mixed[0:CHUNK, :], proj[0:CHUNK, v_cols]).then_inc(v_own2_in, 16)
                for n in range(NW):
                    sp.dma_start(w_raw_part(n), w_out_part(n)).then_inc(w_in[n], 16)
                sp.dma_start(x_io[:, :], x[0:P, :]).then_inc(x_in, 16)
                sp.wait_ge(qk_read, 1)
                load_qk(1)
                body(0, False, True, True)
                body(1, False, True, True)
                with sp.Fori(2, NT - 2) as t:
                    body(t, True, True, True)
                body(NT - 2, True, False, True)
                body(NT - 1, True, False, False)
                store(NT - 2)
                sp.dma_start(x_io[:, :], x[(NT - 1) * P:, :]).then_inc(x_in, 16)
                store(NT - 1)

            @block.scalar
            def _(act):
                def split(n):
                    act.wait_ge(w_in[n], 16)
                    nc.scalar.activation(w_part("hi", n), w_raw_part(n), ACT.Copy).then_inc(w_hi, 1)

                def square_qk(t):
                    act.wait_ge(qk_in, t * 16 + 16)
                    nc.scalar.activation(qn[:, :, :], qk[:, :, :], ACT.Square, scale=HD ** -0.5).then_inc(qk_squared, 1)

                def square_y(t):
                    act.wait_ge(gated, t + 1)
                    nc.scalar.activation(zt, yt, ACT.Square, scale=SSM_W ** -0.5, accum_out=y_ms[:, :]).then_inc(y_squared, 1)

                def exps(t, u, keys):
                    act.wait_ge(ntop_done, t * 2 + u + 1)
                    for n in range(ROWS):
                        nc.scalar.activation(prob[:, u, n, 0:keys], ps_s[:, n, 0:keys], ACT.Exp, bias=ntop[:, u, n:n + 1], scale=SCALE,
                                             accum_out=row_sum[:, u, n:n + 1])
                    nc.scalar.activation(sink_exp[:, u], sink_arg[:, u], ACT.Exp).then_inc(exp_done, 1)

                def copy_probT(t, u, keys):
                    act.wait_ge(prob_turned, t * 2 + u + 1)
                    nc.scalar.activation(probT[0:keys, u], ps_t[0:keys], ACT.Copy).then_inc(probT_done, 1)

                def body(t, first, last):
                    act.wait_ge(q_turned, t + 1)
                    if not first:
                        act.wait_ge(s_mm, t * 2)
                    nc.scalar.activation(qT[:, :, :, :].rearrange("p u b c -> p b u c"), ps_t[:, :, :].rearrange("p b (u c) -> p b u c", u=2), ACT.Copy).then_inc(qT_done, 1)
                    if not last:
                        act.wait_ge(kd_done, t + 1)
                        square_qk(t + 1)
                    keys0 = CHUNK if first else P
                    exps(t, 0, keys0)
                    if first:
                        split(0)
                    exps(t, 1, P)
                    copy_probT(t, 0, keys0)
                    if not last:
                        square_y(t + 1)
                    copy_probT(t, 1, P)
                    act.wait_ge(pv_mm, t * 2 + 2)
                    if not first:
                        act.wait_ge(out_mm, t * 2)
                    nc.scalar.activation(mix["hi"][:, NK:, :], ps_a[:, :, :, :].rearrange("p a b c -> p a (b c)"), ACT.Copy).then_inc(at_hi, 1)
                    act.wait_ge(gained, t + 1)
                    nc.scalar.activation(mix["hi"][:, 0:NK, :], full[:, :, :], ACT.Copy).then_inc(y_hi, 1)
                    if first:
                        for n in range(1, NW):
                            split(n)

                square_qk(0)
                square_y(0)
                tiles(act, body)

            @block.gpsimd
            def _(pool):
                def prepare(t):
                    pool.wait_ge(qk_summed, t + 1)
                    nc.gpsimd.tensor_tensor(qk_rs[:, :], qk_ms[:, :], eps[:, :], ALU.add).then_inc(qk_eps, 1)
                    pool.wait_ge(qk_eps, t + 1)
                    nc.gpsimd.tensor_tensor(qk_rs[:, :], qk_rs[:, :], power[:, :], ALU.pow).then_inc(qk_rs_ready, 1)
                    pool.wait_ge(y_in_, t * 16 + 16)
                    pool.wait_ge(z_in, t * 16 + 16)
                    nc.gpsimd.tensor_tensor(yt, yt, zt, ALU.mult).then_inc(gated, 1)
                    pool.wait_ge(y_squared, t + 1)
                    nc.gpsimd.tensor_tensor(y_rs[:, :], y_ms[:, :], eps[:, 0:1], ALU.add).then_inc(y_eps, 1)
                    pool.wait_ge(y_eps, t + 1)
                    nc.gpsimd.tensor_tensor(y_rs[:, :], y_rs[:, :], power[:, 0:1], ALU.pow).then_inc(y_rs_ready, 1)

                nc.gpsimd.memset(eps[:, :], EPS).then_inc(set_power, 1)
                nc.gpsimd.memset(power[:, :], -0.5).then_inc(set_power, 1)
                pool.wait_ge(set_power, 2)
                prepare(0)
                with pool.Fori(1, NT) as t:
                    prepare(t)

            @block.vector
            def _(dve):
                qc = Chain(dve, qk_step, 2)
                tc = Chain(dve, top_step, 4)
                ic = Chain(dve, inv_step, 4)

                def split(n):
                    dve.wait_ge(w_hi, n + 1)
                    nc.vector.tensor_tensor(w_part("lo", n), w_raw_part(n), w_part("hi", n).bitcast(F32), ALU.subtract).then_inc(w_lo, 1)

                def sum_qk(t):
                    dve.wait_ge(qk_squared, t + 1)
                    nc.vector.tensor_reduce(qk_ms[:, :], qn[:, :, :], AX.X, ALU.add).then_inc(qk_summed, 1)

                def scale_qk(t):
                    qc.turn(t)
                    dve.wait_ge(qk_rs_ready, t + 1)
                    nc.vector.tensor_tensor(qn[:, :, :], qk[:, :, :], spread(qk_rs[:, :], HD), ALU.mult).then_inc(qk_read, 1)
                    dve.wait_ge(qk_read, t + 1)
                    nc.vector.tensor_tensor(qn[:, 0:Q_H, :], qn[:, 0:Q_H, :], repeat(K["gq"][:, :], Q_H), ALU.mult)
                    qc.link(nc.vector.tensor_tensor(qn[:, Q_H:, :], qn[:, Q_H:, :], repeat(K["gk"][:, :], KV_H), ALU.mult))

                def rotate_qk(t, first):
                    cos, sin = (repeat(K[n][:, ds(t, 1), :].rearrange("p o f -> p (o f)"), QK_H) for n in ("cos", "sin"))
                    x1, x2 = qn[:, :, 0:RH], qn[:, :, RH:ROPE]
                    for n, (src, wave) in enumerate(((x1, cos), (x2, sin), (x2, cos), (x1, sin))):
                        ins = nc.vector.tensor_tensor(rope[:, n], src, wave, ALU.mult)
                    qc.link(ins)
                    nc.vector.tensor_tensor(x1, rope[:, 0], rope[:, 1], ALU.subtract)
                    nc.vector.tensor_tensor(x2, rope[:, 2], rope[:, 3], ALU.add).then_inc(qn_done, 1)
                    qc.close()
                    dve.wait_ge(qn_done, t + 1)
                    if not first:
                        dve.wait_ge(k_turned, t)
                    k_heads = qn[:, Q_H:, :].unsqueeze(2).to_broadcast([P, KV_H, 2, HD])
                    nc.vector.tensor_copy(kd[:, :, :, :], k_heads).then_inc(kd_done, 1)

                def scale_y(t):
                    dve.wait_ge(y_rs_ready, t + 1)
                    nc.vector.tensor_scalar(yt, yt, y_rs[:, :], None, ALU.mult).then_inc(y_scaled, 1)

                def add_out(t, half):
                    if half == 0:
                        dve.wait_ge(x_in, t * 16 + 16)
                    dve.wait_ge(out_mm, t * 2 + half + 1)
                    part = x_io[:, half * HALF:(half + 1) * HALF]
                    nc.vector.tensor_tensor(part, ps_o[:, half], part, ALU.add).then_inc(out_added, 1)

                def tops(t, u, keys):
                    dve.wait_ge(s_mm, t * 2 + u + 1)
                    tc.link(nc.vector.tensor_reduce(top[:, u], ps_s[:, :, 0:keys], AX.X, ALU.max))
                    tc.link(nc.vector.scalar_tensor_tensor(ntop[:, u], top[:, u], -SCALE, flat(K["nsink"][:, :, :]), ALU.mult, ALU.min))
                    nc.vector.tensor_tensor(sink_arg[:, u], flat(K["sink"][:, :, :]), ntop[:, u], ALU.add).then_inc(ntop_done, 1)

                def probs(t, u, keys):
                    dve.wait_ge(exp_done, t * 2 + u + 1)
                    ic.link(nc.vector.tensor_tensor(inv[:, u], row_sum[:, u], sink_exp[:, u], ALU.add))
                    ic.link(nc.vector.reciprocal(inv[:, u], inv[:, u]))
                    p = prob[:, u, :, 0:keys]
                    nc.vector.tensor_tensor(p, p, spread(inv[:, u], keys), ALU.mult).then_inc(prob_done, 1)

                def body(t, first, last):
                    tc.turn(t), ic.turn(t)
                    if not first:
                        dve.wait_ge(s_mm, t * 2)
                        nc.vector.tensor_copy(kT[:, :, 2, :], kT[:, :, 1, :]).then_inc(kT_moved, 1)
                        dve.wait_ge(kT_moved, t)
                    dve.wait_ge(k_turned, t + 1)
                    nc.vector.tensor_copy(kT[:, :, 0:2, :], ps_a[:, 0:KV_H]).then_inc(kT_done, 1)
                    if not last:
                        sum_qk(t + 1)
                    dve.wait_ge(y_turned, t + 1)
                    nc.vector.tensor_tensor(full[:, :, :], ps_t[:, :, :], spread(K["pc1"][:, PC_SSM:PC_SSM + NK], P), ALU.mult).then_inc(gained, 1)
                    keys0 = CHUNK if first else P
                    tops(t, 0, keys0)
                    probs(t, 0, keys0)
                    tops(t, 1, P)
                    if not first:
                        add_out(t - 1, 0)
                    else:
                        split(0)
                    if not last:
                        scale_qk(t + 1)
                    probs(t, 1, P)
                    if not last:
                        rotate_qk(t + 1, False)
                        scale_y(t + 1)
                    tc.close(), ic.close()
                    dve.wait_ge(at_hi, t + 1)
                    nc.vector.tensor_tensor(mix["lo"][:, NK:, :], ps_a[:, :, :, :].rearrange("p a b c -> p a (b c)"),
                                            mix["hi"][:, NK:, :].bitcast(F32), ALU.subtract).then_inc(at_lo, 1)
                    dve.wait_ge(y_hi, t + 1)
                    nc.vector.tensor_tensor(mix["lo"][:, 0:NK, :], full[:, :, :], mix["hi"][:, 0:NK, :].bitcast(F32), ALU.subtract).then_inc(y_lo, 1)
                    if not first:
                        add_out(t - 1, 1)
                    else:
                        for n in range(1, NW):
                            split(n)

                sum_qk(0)
                scale_qk(0)
                rotate_qk(0, True)
                scale_y(0)
                tiles(dve, body)
                for half in range(2):
                    add_out(NT - 1, half)

            @block.tensor
            def _(pe):
                def project(t, half, part):
                    if half == 0:
                        pe.wait_ge(y_lo if part else at_lo, t + 1)
                    pe.wait_ge(w_lo, (half * 2 + part + 1) * NW // 4)
                    cols = slice(half * HALF, (half + 1) * HALF)
                    for n in range(NK):
                        m = n if part else NK + n
                        ins = product(nc, ps_o[:, half], {p: mix[p][:, m, :] for p in w}, {p: w[p][:, m, cols] for p in w},
                                      n == 0 and not part, n == NK - 1 and part == 1)
                    if part:
                        ins.then_inc(out_mm, 1)

                def scores(t, u, first):
                    if u == 0:
                        pe.wait_ge(qT_done, t + 1)
                        pe.wait_ge(kT_done, t + 1)
                        if not first:
                            pe.wait_ge(exp_done, t * 2)
                    else:
                        pe.wait_ge(exp_done, t * 2 + 1)
                    for c in range(2):
                        rows = slice(c * HD, (c + 1) * HD)
                        for j in range(KV_H):
                            if u:
                                keys = kT[rows, j, 0:2, :]
                            else:
                                keys = kT[rows, j, 0:1, :] if first else kT[rows, j, 0:3:2, :]
                            n = CHUNK if first and not u else P
                            ins = nc.tensor.matmul(ps_s[:, c * KV_H + j, 0:n], qT[rows, u, 2 * j:2 * j + 2, :].rearrange("p a b -> p (a b)"), keys, start=True, stop=True)
                    ins.then_inc(s_mm, 1)

                def turn_probs(t, u, first):
                    pe.wait_ge(prob_done, t * 2 + u + 1)
                    if u:
                        pe.wait_ge(probT_done, t * 2 + 1)
                    else:
                        pe.wait_ge(gained, t + 1)
                    n = CHUNK if first and not u else P
                    for m in range(ROWS):
                        ins = nc.tensor.transpose(ps_t[0:n, m, :], prob[:, u, m, 0:n], K["ident"][:, :])
                    ins.then_inc(prob_turned, 1)

                def values(t, u, first):
                    pe.wait_ge(probT_done, t * 2 + u + 1)
                    if u:
                        pe.wait_ge(v_own_in, t * 16 + 16)
                        v = v_own[:, :]
                    else:
                        pe.wait_ge(v_own2_in, t * 16 + 16)
                        if not first:
                            pe.wait_ge(v_before_in, t * 16)
                        v = v_mixed[0:CHUNK if first else P, :]
                    n = v.shape[0]
                    for c in range(2):
                        for j in range(KV_H):
                            ins = nc.tensor.matmul(ps_a[c * HD:(c + 1) * HD, 2 * j:2 * j + 2, u, :], v[:, j * HD:(j + 1) * HD],
                                                   probT[0:n, u, c * KV_H + j, :], start=True, stop=True)
                    ins.then_inc(pv_mm, 1)

                def body(t, first, last):
                    pe.wait_ge(qn_done, t + 1)
                    if not first:
                        pe.wait_ge(probT_done, t * 2)
                    for b in range(NQB):
                        ins = nc.tensor.transpose(ps_t[:, b, :], qn[:, 2 * b:2 * b + 2, :].rearrange("p a b -> p (a b)"), K["ident"][:, :])
                    ins.then_inc(q_turned, 1)
                    pe.wait_ge(kd_done, t + 1)
                    if not first:
                        pe.wait_ge(at_lo, t)
                    for j in range(KV_H):
                        ins = nc.tensor.transpose(ps_a[:, j].rearrange("p a b -> p (a b)"), kd[:, j].rearrange("p a b -> p (a b)"), K["ident"][:, :])
                    ins.then_inc(k_turned, 1)
                    if not first:
                        project(t - 1, 0, 0)
                    pe.wait_ge(y_scaled, t + 1)
                    pe.wait_ge(qT_done, t + 1)
                    for b in range(NK):
                        ins = nc.tensor.transpose(ps_t[:, b, :], yt[:, b * P:(b + 1) * P], K["ident"][:, :])
                    ins.then_inc(y_turned, 1)
                    scores(t, 0, first)
                    if not first:
                        project(t - 1, 0, 1)
                    scores(t, 1, first)
                    turn_probs(t, 0, first)
                    if not first:
                        project(t - 1, 1, 0)
                    values(t, 0, first)
                    turn_probs(t, 1, first)
                    if not first:
                        project(t - 1, 1, 1)
                    values(t, 1, first)

                tiles(pe, body)
                project(NT - 1, 0, 0)
                project(NT - 1, 0, 1)
                pe.wait_ge(out_added, (NT - 1) * 2)
                project(NT - 1, 1, 0)
                project(NT - 1, 1, 1)
        r.clear()


def ffn_stage(nc, a, K, hT, x_sb, out):
    w_in = a["w_ffn_in"].rearrange("o (k p) c -> p (o k) c", p=P)
    w_down = a["w_ffn_out"].rearrange("o (f p) c -> p (o f) c", p=P)
    LEAD = FFN_CONV - 1
    NPART = 2 * GF
    NOUT = 2 * NT
    with ExitStack() as ctx:
        r = Room(nc, ctx, "ffn")
        raw = r.sb("raw", [P, 2, NK, P])
        w = {part: r.sb(f"w_{part}", [P, NPART, NK, P], F32R) for part in ("hi", "lo")}
        down_raw = r.sb("down_raw", [P, GF, D])
        down = {part: r.sb(f"down_{part}", [P, GF, D], F32R) for part in ("hi", "lo")}
        pre = r.sb("pre", [P, LEAD + L])
        conv = r.sb("conv", [P, L])
        hid = {part: r.sb(f"hid_{part}", [P, GF, L], F32R) for part in ("hi", "lo")}
        ps_in = r.ps("ps_in", [P, 2, 2, HALF])
        ps_out = r.ps("ps_out", [P, 4, HALF])
        raw_in = [r.sem(f"raw_in{u}") for u in range(2)]
        down_in, padded = r.sem("down_in"), r.sem("padded")
        w_hi, w_lo, down_hi, down_lo = r.sem("w_hi"), r.sem("w_lo"), r.sem("down_hi"), r.sem("down_lo")
        in_mm, evac, conv_step, conv_done, silu = r.sem("in_mm"), r.sem("evac"), r.sem("conv_step"), r.sem("conv_done"), r.sem("silu")
        hid_done, hid_hi, hid_lo = r.sem("hid_done"), r.sem("hid_hi"), r.sem("hid_lo")
        out_mm, added, x_out = r.sem("out_mm"), r.sem("added"), r.sem("x_out")

        def groups(eng, body):
            body(0, True, False)
            with eng.Fori(1, NG - 1) as g:
                body(g, False, False)
            body(NG - 1, False, True)

        with nc.Block() as block:

            @block.sync
            def _(sp):
                def body(g, first, last):
                    for q in range(NPART):
                        if not (first and q < 2):
                            sp.wait_ge(w_hi, g * NPART + q - 1)
                            sp.wait_ge(w_lo, g * NPART + q - 1)
                        col = g * (GF * P) + (q // 2) * P + (q % 2) * D_FF
                        sp.dma_start(raw[:, q % 2], w_in[:, :, ds(col, P)]).then_inc(raw_in[q % 2], 16)
                        if q == 1:
                            if not first:
                                sp.wait_ge(down_lo, g)
                            sp.dma_start(down_raw[:, :, :], w_down[:, ds(g * GF, GF), :]).then_inc(down_in, 16)

                groups(sp, body)
                for t in range(NT):
                    sp.wait_ge(added, (NG - 1) * NOUT + 2 * t + 2)
                    sp.dma_start(out[t * P:(t + 1) * P, :], x_sb[:, t, :]).then_inc(x_out, 16)
                sp.wait_ge(x_out, 16 * NT)

            @block.scalar
            def _(act):
                def split(g, q, first):
                    act.wait_ge(raw_in[q % 2], g * 32 + 16 * (q // 2) + 16)
                    if not first:
                        act.wait_ge(in_mm, (g - 1) * NPART + q + 1)
                    nc.scalar.activation(w["hi"][:, q], raw[:, q % 2], ACT.Copy).then_inc(w_hi, 1)

                def body(g, first, last):
                    for c in range(GF):
                        if c == 0:
                            split(g, 2, first)
                            split(g, 3, first)
                        act.wait_ge(in_mm, g * NPART + 2 * c + 1)
                        if first and c == 0:
                            act.wait_ge(padded, 1)
                        else:
                            act.wait_ge(conv_done, g * GF + c)
                        nc.scalar.activation(pre[:, LEAD:], ps_in[:, 0].rearrange("p a b -> p (a b)"), ACT.Copy).then_inc(evac, 1)
                        if c == 1:
                            act.wait_ge(down_in, g * 16 + 16)
                            if not first:
                                act.wait_ge(out_mm, g * NOUT)
                            nc.scalar.activation(down["hi"][:, :, :], down_raw[:, :, :], ACT.Copy).then_inc(down_hi, 1)
                        act.wait_ge(conv_done, g * GF + c + 1)
                        nc.scalar.activation(conv[:, :], conv[:, :], ACT.Silu).then_inc(silu, 1)
                        if c == 1 and not last:
                            split(g + 1, 0, False)
                            split(g + 1, 1, False)
                        act.wait_ge(hid_done, g * GF + c + 1)
                        if not first:
                            act.wait_ge(out_mm, g * NOUT)
                        nc.scalar.activation(hid["hi"][:, c], conv[:, :], ACT.Copy).then_inc(hid_hi, 1)

                split(0, 0, True)
                split(0, 1, True)
                groups(act, body)

            @block.vector
            def _(dve):
                cc = Chain(dve, conv_step, GF * (FFN_CONV - 1))

                def split(g, q, first):
                    dve.wait_ge(w_hi, g * NPART + q + 1)
                    nc.vector.tensor_tensor(w["lo"][:, q], raw[:, q % 2], w["hi"][:, q].bitcast(F32), ALU.subtract).then_inc(w_lo, 1)

                def add(g, n):
                    dve.wait_ge(out_mm, g * NOUT + n + 1)
                    part = x_sb[:, n // 2, (n % 2) * HALF:(n % 2 + 1) * HALF]
                    nc.vector.tensor_tensor(part, ps_out[:, n % 4], part, ALU.add).then_inc(added, 1)

                def body(g, first, last):
                    cc.turn(g)
                    for c in range(GF):
                        if c == 0:
                            split(g, 2, first)
                            split(g, 3, first)
                        f = g * GF + c
                        tap = lambda j: K["pc2"][:, ds(f + j * NF, 1)]
                        dve.wait_ge(evac, f + 1)
                        if not (first and c == 0):
                            dve.wait_ge(hid_hi, f)
                            dve.wait_ge(hid_lo, f)
                        cc.link(nc.vector.tensor_scalar(conv[:, :], pre[:, LEAD:], tap(LEAD), K["pc2"][:, ds(f + PC_FB, 1)], ALU.mult, ALU.add))
                        cc.link(nc.vector.scalar_tensor_tensor(conv[:, :], pre[:, 1:1 + L], tap(1), conv[:, :], ALU.mult, ALU.add))
                        nc.vector.scalar_tensor_tensor(conv[:, :], pre[:, 0:L], tap(0), conv[:, :], ALU.mult, ALU.add).then_inc(conv_done, 1)
                        if c == 1:
                            dve.wait_ge(down_hi, g + 1)
                            nc.vector.tensor_tensor(down["lo"][:, :, :], down_raw[:, :, :], down["hi"][:, :, :].bitcast(F32), ALU.subtract).then_inc(down_lo, 1)
                            if not last:
                                split(g + 1, 0, False)
                                split(g + 1, 1, False)
                        dve.wait_ge(silu, f + 1)
                        dve.wait_ge(in_mm, g * NPART + 2 * c + 2)
                        nc.vector.tensor_tensor(conv[:, :], ps_in[:, 1].rearrange("p a b -> p (a b)"), conv[:, :], ALU.mult).then_inc(hid_done, 1)
                        dve.wait_ge(hid_hi, f + 1)
                        nc.vector.tensor_tensor(hid["lo"][:, c], conv[:, :], hid["hi"][:, c].bitcast(F32), ALU.subtract).then_inc(hid_lo, 1)
                    cc.close()
                    for n in range(NOUT):
                        add(g, n)

                nc.vector.memset(pre[:, 0:LEAD], 0.0).then_inc(padded, 1)
                split(0, 0, True)
                split(0, 1, True)
                groups(dve, body)

            @block.tensor
            def _(pe):
                def project(g, q, first):
                    c, kind = q // 2, q % 2
                    pe.wait_ge(w_lo, g * NPART + q + 1)
                    if not first:
                        pe.wait_ge(hid_done if kind else evac, g * GF + c)
                    for half in range(2):
                        for k in range(NK):
                            ins = product(nc, ps_in[:, kind, half], {p: w[p][:, q, k, :] for p in w},
                                          {p: hT[p][:, k, half * HALF:(half + 1) * HALF] for p in w}, k == 0, k == NK - 1)
                    ins.then_inc(in_mm, 1)

                def body(g, first, last):
                    for q in range(1, NPART):
                        project(g, q, first and q == 1)
                    if not last:
                        project(g + 1, 0, False)
                    pe.wait_ge(hid_lo, (g + 1) * GF)
                    pe.wait_ge(down_lo, g + 1)
                    for n in range(NOUT):
                        t, half = n // 2, n % 2
                        if n >= 4:
                            pe.wait_ge(added, g * NOUT + n - 3)
                        elif not first:
                            pe.wait_ge(added, g * NOUT + n - 3)
                        for c in range(GF):
                            ins = product(nc, ps_out[:, n % 4], {p: hid[p][:, c, t * P:(t + 1) * P] for p in w},
                                          {p: down[p][:, c, half * HALF:(half + 1) * HALF] for p in w}, c == 0, c == GF - 1)
                        ins.then_inc(out_mm, 1)

                project(0, 0, True)
                groups(pe, body)


def build(nc, a, out):
    xbcT = nc.dram_tensor("xbcT_scratch", [XBC_W, L], F32, kind="Internal").ap()
    proj = nc.dram_tensor("proj_scratch", [L, SSM_W + QK_H * HD + KV_W], F32, kind="Internal").ap()
    y = nc.dram_tensor("y_scratch", [L, SSM_W], F32, kind="Internal").ap()
    x_new = nc.dram_tensor("x_new_scratch", [L, D], F32, kind="Internal").ap()
    with ExitStack() as ctx:
        keep = Room(nc, ctx, "keep")
        K = constants(nc, keep, a)
        with ExitStack() as first:
            r = Room(nc, first, "in")
            S = {n: r.sb(n, [P, NT, SSM_H]) for n in ("dt", "dA", "nacs", "eacs", "cdec", "wend")}
            hT = {part: r.sb(f"hT_{part}", [P, NK, L], F32R) for part in ("hi", "lo")}
            with nc.sbuf_tensor("x_sb", [P, NT, D], F32) as x_sb:
                norm_stage(nc, "norm_mix", a["x"].rearrange("o t d -> (o t) d"), PC_MIX, K, x_sb, hT)
            xbc_stage(nc, a, K, hT, xbcT, S)
            scan_stage(nc, a, K, hT, xbcT, S, proj, y)
        mix_stage(nc, a, K, proj, y, x_new)
        with ExitStack() as second:
            r = Room(nc, second, "up")
            hT = {part: r.sb(f"hT_{part}", [P, NK, L], F32R) for part in ("hi", "lo")}
            x_sb = r.sb("x_sb", [P, NT, D])
            norm_stage(nc, "norm_ffn", x_new, PC_FFN, K, x_sb, hT)
            ffn_stage(nc, a, K, hT, x_sb, out.rearrange("o t d -> (o t) d"))


_INS = ['x', 'positions', 'norm_mix', 'w_in', 'conv_w', 'conv_b', 'dt_bias', 'a_log', 'd_skip', 'ssm_norm',
        'q_norm', 'k_norm', 'sinks', 'w_out', 'norm_ffn', 'w_ffn_in', 'ffn_conv_w', 'ffn_conv_b', 'w_ffn_out']


def kernel(**inputs):
    import concourse.bacc as _bacc
    from concourse.bass_utils import run_bass_kernel_spmd as _run

    nc = _bacc.Bacc("TRN2", target_bir_lowering=False, num_devices=1)
    arrays, args = {}, {}
    for name in _INS:
        v = np.ascontiguousarray(inputs[name])
        arrays[f"in_{name}"] = v
        args[name] = nc.dram_tensor(f"in_{name}", v.shape, mybir.dt.from_np(v.dtype), kind="ExternalInput").ap()
    out = nc.dram_tensor("out_x", [1, L, D], F32, kind="ExternalOutput").ap()
    build(nc, args, out)
    r = _run(nc, [arrays], core_ids=[0])
    return r.results[0]["out_x"]
```

```python
from contextlib import ExitStack

import numpy as np

import concourse.bass as bass
from concourse import mybir

F32 = mybir.dt.float32
F32R = mybir.dt.float32r
I32 = mybir.dt.int32
ACT = mybir.ActivationFunctionType
ALU = mybir.AluOpType
AX = mybir.AxisListType
ds = bass.ds

P = 128
L = 1024
D = 1024
NT = L // P
NK = D // P
HALF = 512
EPS = 1e-6

SSM_H, SSM_P, SSM_G, STATE, SSM_CONV = 16, 64, 2, 128, 4
SSM_W = SSM_H * SSM_P
HPG = SSM_H // SSM_G
XBC_W = SSM_W + 2 * SSM_G * STATE
NB_XBC = XBC_W // P
Q_H, KV_H, HD = 16, 4, 64
QK_H = Q_H + KV_H
CHUNK = 64
ROPE = HD // 4
RH = ROPE // 2
THETA = 500000.0
SCALE = HD ** -0.5
Z0 = 0
XBC0 = SSM_W
DT0 = XBC0 + XBC_W
Q0 = DT0 + SSM_H
KV0 = Q0 + Q_H * HD
KV_W = KV_H * HD
IN_W = KV0 + 2 * KV_W
MIX_W = SSM_W + Q_H * HD
NM = MIX_W // P
D_FF = 2816
NF = D_FF // P
FFN_CONV = 3
GF = 2
NG = NF // GF
PB = 256
BIG = 1e30

PC_MIX, PC_FFN, PC_SSM, PC_CW = 0, NK, 2 * NK, 3 * NK
PC_CB = PC_CW + SSM_CONV * NB_XBC
PC1 = PC_CB + NB_XBC
PC_FB = FFN_CONV * NF
PC2 = PC_FB + NF

PASSES = (("hi", "hi"), ("hi", "lo"), ("lo", "hi"))


class Room:

    def __init__(self, nc, ctx, stage):
        self.nc, self.ctx, self.stage, self.sems = nc, ctx, stage, []

    def sb(self, name, shape, dt=F32):
        return self.ctx.enter_context(self.nc.sbuf_tensor(f"{self.stage}_{name}", shape, dt))

    def ps(self, name, shape):
        return self.ctx.enter_context(self.nc.psum_tensor(f"{self.stage}_{name}", shape, F32))

    def sem(self, name):
        self.sems.append(self.nc.alloc_semaphore(f"{self.stage}_{name}"))
        return self.sems[-1]

    def clear(self, *others):
        self.nc.clear_and_free_semaphores(sum((o.sems for o in others), self.sems))
        self.nc.all_engine_barrier()


class Chain:

    def __init__(self, eng, sem, per=0):
        self.eng, self.sem, self.per, self.base, self.n = eng, sem, per, 0, 0

    def turn(self, i):
        self.base, self.n = i * self.per, 0

    def link(self, ins):
        ins.then_inc(self.sem, 1)
        self.n += 1
        self.eng.wait_ge(self.sem, self.base + self.n)

    def close(self):
        assert self.n == self.per, (self.n, self.per)


def spread(ap, n):
    return ap.unsqueeze(2).to_broadcast([ap.shape[0], ap.shape[1], n])


def repeat(ap, n):
    return ap.unsqueeze(1).to_broadcast([ap.shape[0], n, ap.shape[1]])


def constant_tiles(keep):
    K = {}
    K["ident"] = keep.sb("ident", [P, P])
    K["tri"] = keep.sb("tri", [P, P])
    K["cap"] = keep.sb("cap", [P, P])
    K["ones"] = keep.sb("ones", [P, P])
    K["pc1"] = keep.sb("pc1", [P, PC1])
    K["pc2"] = keep.sb("pc2", [P, PC2])
    K["dtb"] = keep.sb("dtb", [P, SSM_H])
    K["alog"] = keep.sb("alog", [P, SSM_H])
    K["dskip"] = keep.sb("dskip", [P, SSM_H])
    K["gq"] = keep.sb("gq", [P, HD])
    K["gk"] = keep.sb("gk", [P, HD])
    K["sink"] = keep.sb("sink", [P, 2, KV_H])
    K["nsink"] = keep.sb("nsink", [P, 2, KV_H])
    K["sin"] = keep.sb("sin", [P, NT, RH])
    K["cos"] = keep.sb("cos", [P, NT, RH])
    return K


def constants(nc, r, a, K, psT):
    rows1, rows2 = r.sb("rows1", [PC1, P]), r.sb("rows2", [PC2, P])
    posi, posf = r.sb("posi", [NT, P], I32), r.sb("posf", [NT, P])
    pos = r.sb("pos", [P, NT])
    ang, turns = r.sb("ang", [P, NT, RH]), r.sb("turns", [P, 2, NT, RH])
    rest = r.sb("rest", [P, 2, NT, RH])
    rows_in, loaded, made, filled = r.sem("rows_in"), r.sem("loaded"), r.sem("made"), r.sem("filled")
    turned, columns = r.sem("const_turned"), r.sem("columns")
    pos_ready, pos_copied, angles, steps = r.sem("pos_ready"), r.sem("pos_copied"), r.sem("angles"), r.sem("steps")
    waves = r.sem("waves")
    loads = []

    def row_load(dst, src):
        loads.append((dst, src))

    row_load(rows1[PC_MIX:PC_MIX + NK, :], a["norm_mix"].rearrange("o (k p) -> (o k) p", p=P))
    row_load(rows1[PC_FFN:PC_FFN + NK, :], a["norm_ffn"].rearrange("o (k p) -> (o k) p", p=P))
    row_load(rows1[PC_SSM:PC_SSM + NK, :], a["ssm_norm"].rearrange("o (k p) -> (o k) p", p=P))
    row_load(rows1[PC_CW:PC_CB, :], a["conv_w"].rearrange("o j (k p) -> (o j k) p", p=P))
    row_load(rows1[PC_CB:PC1, :], a["conv_b"].rearrange("o (k p) -> (o k) p", p=P))
    row_load(rows2[0:PC_FB, :], a["ffn_conv_w"].rearrange("o j (k p) -> (o j k) p", p=P))
    row_load(rows2[PC_FB:PC2, :], a["ffn_conv_b"].rearrange("o (k p) -> (o k) p", p=P))
    row_load(posi[:, :], a["positions"].rearrange("o (t p) -> (o t) p", p=P))
    N_ROWS = len(loads)
    for name, src in (("dtb", "dt_bias"), ("alog", "a_log"), ("dskip", "d_skip"), ("gq", "q_norm"), ("gk", "k_norm")):
        row_load(K[name][:, :], a[src].to_broadcast([P, a[src].shape[1]]))
    by_row = a["sinks"].rearrange("o (j i c) -> o i c j", j=KV_H, i=2)
    for i in range(2):
        for c in range(2):
            row_load(K["sink"][i * CHUNK:(i + 1) * CHUNK, c, :], by_row[:, i, c, :].to_broadcast([CHUNK, KV_H]))

    def sync(sp, start, end):
        with nc.allow_non_contiguous_dma(reason="sixteen sinks"):
            for n in range(start, end):
                sp.dma_start(*loads[n]).then_inc(rows_in if n < N_ROWS else loaded, 16)

    def gpsimd(pool):
        nc.gpsimd.memset(K["ident"][:, :], 0.0).then_inc(filled, 1)
        nc.gpsimd.memset(K["tri"][:, :], 1.0).then_inc(filled, 1)
        nc.gpsimd.memset(K["cap"][:, :], BIG).then_inc(filled, 1)
        nc.gpsimd.memset(K["ones"][:, :], 1.0).then_inc(filled, 1)
        pool.wait_ge(filled, 4)
        nc.gpsimd.affine_select(out=K["ident"][:, :], in_=K["ident"][:, :], compare_op=ALU.not_equal, fill=1.0,
                                base=0, pattern=[[-1, P]], channel_multiplier=1).then_inc(made, 1)
        for m, fill in (("tri", 0.0), ("cap", -BIG)):
            nc.gpsimd.affine_select(out=K[m][:, :], in_=K[m][:, :], compare_op=ALU.is_ge, fill=fill,
                                    base=0, pattern=[[1, P]], channel_multiplier=-1).then_inc(made, 1)

    def tensor(pe):
        pe.wait_ge(rows_in, 16 * N_ROWS)
        pe.wait_ge(made, 1)
        nc.tensor.transpose(psT[:, 0:PC1], rows1[:, :], K["ident"][0:PC1, 0:PC1]).then_inc(turned, 1)
        nc.tensor.transpose(psT[:, P:P + PC2], rows2[:, :], K["ident"][0:PC2, 0:PC2]).then_inc(turned, 1)
        pe.wait_ge(pos_ready, 1)
        nc.tensor.transpose(psT[:, 2 * P:2 * P + NT], posf[:, :], K["ident"][0:NT, 0:NT]).then_inc(turned, 1)

    def vector(dve):
        dve.wait_ge(rows_in, 16 * N_ROWS)
        nc.vector.tensor_copy(posf[:, :], posi[:, :]).then_inc(pos_ready, 1)
        dve.wait_ge(turned, 3)
        nc.vector.tensor_copy(pos[:, :], psT[:, 2 * P:2 * P + NT]).then_inc(pos_copied, 1)
        nc.vector.tensor_copy(K["pc1"][:, :], psT[:, 0:PC1]).then_inc(columns, 1)
        nc.vector.tensor_copy(K["pc2"][:, :], psT[:, P:P + PC2]).then_inc(columns, 1)

    def vector_waves(dve):
        c = Chain(dve, steps)
        dve.wait_ge(loaded, 16 * (len(loads) - N_ROWS))
        nc.vector.tensor_scalar(K["nsink"][:, :, :], K["sink"][:, :, :], -1.0, None, ALU.mult)
        dve.wait_ge(pos_copied, 1)
        inv_freq = np.float32(THETA) ** (-np.arange(0, ROPE, 2, dtype=np.float32) / np.float32(ROPE))
        for f in range(RH):
            ins = nc.vector.tensor_scalar(ang[:, :, f], pos[:, :], float(inv_freq[f]), None, ALU.mult)
        c.link(ins)
        nearest = 1.5 * 2.0 ** 23
        for w, ahead in enumerate((0.0, 0.25)):
            c.link(nc.vector.tensor_scalar(turns[:, w], ang[:, :, :], float(1 / (2 * np.pi)), ahead, ALU.mult, ALU.add))
            c.link(nc.vector.tensor_scalar(turns[:, w], turns[:, w], nearest, None, ALU.add))
            c.link(nc.vector.tensor_scalar(turns[:, w], turns[:, w], nearest, None, ALU.subtract))
            left, src = 2 * np.pi, ang[:, :, :]
            for part in range(4):
                m, e = np.frexp(left)
                piece = float(np.ldexp(np.floor(m * 256) / 256, e)) if part < 3 else float(np.float32(left))
                left -= piece
                c.link(nc.vector.scalar_tensor_tensor(rest[:, w], turns[:, w], -piece, src, ALU.mult, ALU.add))
                src = rest[:, w]
            if w:
                c.link(nc.vector.tensor_scalar(rest[:, w], rest[:, w], float(np.pi / 2), None, ALU.add))
            nc.vector.tensor_scalar(rest[:, w], rest[:, w], 3.1415925, -3.1415925, ALU.min, ALU.max).then_inc(angles, 1)

    def scalar_waves(act):
        act.wait_ge(angles, 1)
        nc.scalar.activation(K["sin"][:, :, :], rest[:, 0], ACT.Sin).then_inc(waves, 1)
        act.wait_ge(angles, 2)
        nc.scalar.activation(K["cos"][:, :, :], rest[:, 1], ACT.Sin).then_inc(waves, 1)

    return {"sync": sync, "made": made, "loads": (N_ROWS, len(loads)), "gpsimd": gpsimd, "tensor": tensor, "vector": vector,
            "vector_waves": vector_waves, "scalar_waves": scalar_waves}


def norm(nc, r, src, gain, K, x_sb, hT, psT, xn, full, junk=None, rstd=None):
    given = rstd is not None
    by_scalar = lambda t: given or t % 2 == 1
    if not given:
        ssq, rstd, power = r.sb("ssq", [P, NT]), r.sb("rstd", [P, NT]), r.sb("power", [P, 1])
    x_in = [r.sem(f"x_in{t}") for t in range(NT)]
    squared, meaned, rstd_ready = r.sem("squared"), r.sem("meaned"), r.sem("rstd_ready")
    scaled = {True: r.sem("scaled_act"), False: r.sem("scaled_dve")}
    turned, gained = r.sem("turned"), r.sem("gained")
    hi_done, lo_done, set_power = r.sem("hi_done"), r.sem("lo_done"), r.sem("set_power")

    def load(eng, t):
        eng.dma_start(x_sb[:, t, :], src[t * P:(t + 1) * P, :]).then_inc(x_in[t], 16)

    def scalar(act, at_half):
        def square(t):
            act.wait_ge(x_in[t], 16)
            if t:
                act.wait_ge(squared, t)
            nc.scalar.activation(junk, x_sb[:, t, :], ACT.Square, accum_out=ssq[:, t:t + 1]).then_inc(squared, 1)

        def scale(t):
            if given:
                act.wait_ge(x_in[t], 16)
            else:
                act.wait_ge(rstd_ready, t + 1)
            if t >= 2:
                act.wait_ge(turned, t - 1)
            nc.scalar.activation(xn[t % 2], x_sb[:, t, :], ACT.Copy, scale=rstd[:, t:t + 1]).then_inc(scaled[True], 1)

        if given:
            scale(0)
            scale(1)
        else:
            square(0)
            square(1)
            scale(1)
            square(2)
        for t in range(NT):
            if t + 3 < NT and not given:
                square(t + 3)
            if t == NT // 2 - 2:
                at_half()
            act.wait_ge(gained, t + 1)
            nc.scalar.activation(hT["hi"][:, :, t * P:(t + 1) * P], full[t % 2], ACT.Copy).then_inc(hi_done, 1)
            if t + 2 < NT and by_scalar(t + 2):
                scale(t + 2)

    def gpsimd(pool):
        nc.gpsimd.memset(power[:, :], -0.5).then_inc(set_power, 1)
        pool.wait_ge(set_power, 1)
        for t in range(NT):
            one = slice(t, t + 1)
            pool.wait_ge(squared, t + 1)
            nc.gpsimd.tensor_scalar(rstd[:, one], ssq[:, one], 1.0 / D, EPS, ALU.mult, ALU.add).then_inc(meaned, 1)
            pool.wait_ge(meaned, t + 1)
            nc.gpsimd.tensor_tensor(rstd[:, one], rstd[:, one], power[:, :], ALU.pow).then_inc(rstd_ready, 1)

    def vector(dve, at_half):
        def scale(t):
            dve.wait_ge(rstd_ready, t + 1)
            if t >= 2:
                dve.wait_ge(turned, t - 1)
            nc.vector.tensor_scalar(xn[0], x_sb[:, t, :], rstd[:, t:t + 1], None, ALU.mult).then_inc(scaled[False], 1)

        def low(t):
            dve.wait_ge(gained, t + 1)
            dve.wait_ge(hi_done, t + 1)
            nc.vector.tensor_tensor(hT["lo"][:, :, t * P:(t + 1) * P], full[t % 2],
                                    hT["hi"][:, :, t * P:(t + 1) * P].bitcast(F32), ALU.subtract).then_inc(lo_done, 1)

        if not by_scalar(0):
            scale(0)
        for t in range(NT):
            if t == NT // 2:
                at_half()
            dve.wait_ge(turned, t + 1)
            if t >= 2:
                dve.wait_ge(lo_done, t - 1)
            nc.vector.tensor_tensor(full[t % 2], psT[t % 2], spread(K["pc1"][:, gain:gain + NK], P), ALU.mult).then_inc(gained, 1)
            if t + 2 < NT and not by_scalar(t + 2):
                scale(t + 2)
            if t:
                low(t - 1)
        low(NT - 1)

    def tensor(pe, t):
        pe.wait_ge(scaled[by_scalar(t)], t + 1 if given else t // 2 + 1)
        if t >= 2:
            pe.wait_ge(gained, t - 1)
        for k in range(NK):
            ins = nc.tensor.transpose(psT[t % 2][:, k, :], xn[t % 2][:, k * P:(k + 1) * P], K["ident"][:, :])
        ins.then_inc(turned, 1)

    return {"load": load, "scalar": scalar, "gpsimd": gpsimd, "vector": vector, "tensor": tensor, "turned": turned, "gained": gained, "lo_done": lo_done}


def product(nc, out, w, h, first, last):
    for n, (a, b) in enumerate(PASSES):
        ins = nc.tensor.matmul(out, w[a], h[b], start=first and n == 0, stop=last and n == len(PASSES) - 1)
    return ins


def xbc(nc, r, a, K, hT, xbcT, S, mem, kv):
    w_in = a["w_in"].rearrange("o (k p) c -> p (o k) c", p=P)
    raw, w, ps, ps_dt, ps_sum, dtT = mem["raw_xbc"], mem["w"], mem["ps_xbc"], mem["ps_dt"], mem["ps_sum"], mem["dtT"]
    act_out, ps_dtT = mem["act_out"], mem["ps_t"][0:2 * SSM_H, :, :].rearrange("p (a b) c -> p a (b c)", a=2)
    wdt_raw = r.sb("wdt_raw", [P, NK, SSM_H])
    dA = mem["dA"]
    wdt_both = r.sb("wdt", [P, NK, 2, SSM_H], F32R)
    wdt = {"hi": wdt_both[:, :, 0, :], "lo": wdt_both[:, :, 1, :]}
    pre, conv = mem["pre"], mem["conv"]
    decays_made, dt_copied, dt_turned = r.sem("decays_made"), r.sem("dt_copied"), r.sem("dt_turned")
    const = constants(nc, r, a, K, mem["ps_const"])
    nm = norm(nc, r, a["x"].rearrange("o t d -> (o t) d"), PC_MIX, K, mem["x_sb"], hT,
              [mem["ps_t"], ps[:, 1].rearrange("p a (b c) -> p (a b) c", c=P)],
              [mem["xn"][:, 0], mem["xn"][:, 1]], [mem["full"][:, 0], mem["full"][:, 1]], junk=mem["junk"])
    t1, t2, t3, t4 = mem["t4"]
    ea = r.sb("ea", [P, SSM_H])
    raw_in = [r.sem(f"raw_in{u}") for u in range(2)]
    stored = [r.sem(f"stored{u}") for u in range(2)]
    dt_in, dt_hi, dt_lo = r.sem("dt_in"), r.sem("dt_hi"), r.sem("dt_lo")
    w_hi, w_lo, mm, evac = r.sem("w_hi"), r.sem("w_lo"), r.sem("mm"), r.sem("evac")
    padded, conv_step, conv_done, silu = r.sem("padded"), r.sem("conv_step"), r.sem("conv_done"), r.sem("silu")
    dt_mm, dve_dt, act_dt, da_ready, sums = r.sem("dt_mm"), r.sem("dve_dt"), r.sem("act_dt"), r.sem("da_ready"), r.sem("sums")
    NP_ = NB_XBC // 2

    def sync(sp):
        def load_block(b, u):
            sp.dma_start(raw[:, u], w_in[:, :, ds(b * P + XBC0, P)]).then_inc(raw_in[u], 16)

        n_rows, n_loads = const["loads"]
        nm["load"](sp, 0)
        const["sync"](sp, 0, n_rows)
        for t in range(1, NT):
            nm["load"](sp, t)
            if t == NT // 2:
                sp.dma_start(wdt_raw[:, :, :], w_in[:, :, DT0:DT0 + SSM_H]).then_inc(dt_in, 16)
                load_block(0, 0)
        const["sync"](sp, n_rows, n_loads)

        def body(i, first, last):
            for u in range(2):
                b = i * 2 + u
                if not first:
                    sp.wait_ge(w_hi, b - 1)
                    sp.wait_ge(w_lo, b - 1)
                if last and u == 0:
                    kv["sync"](sp, 0)
                if not (first and u == 0):
                    load_block(b, u)

        body(0, True, False)
        with sp.Fori(1, NP_ - 1) as i:
            body(i, False, False)
        body(NP_ - 1, False, True)

    def scalar(act):
        def split(b, u):
            act.wait_ge(raw_in[u], (b - u) * 8 + 16)
            nc.scalar.activation(w["hi"][:, 1, :, u * P:(u + 1) * P], raw[:, u], ACT.Copy).then_inc(w_hi, 1)

        def body(i, first, last):
            for u in range(2):
                b = i * 2 + u
                act.wait_ge(mm, b + 1)
                if not (first and u == 0):
                    act.wait_ge(conv_done, b)
                else:
                    act.wait_ge(padded, 1)
                nc.scalar.activation(pre[:, SSM_CONV - 1:], ps[:, u].rearrange("p a b -> p (a b)"), ACT.Copy).then_inc(evac, 1)
                if not last:
                    split(b + 2, u)
                else:
                    kv["scalar"](act, u)
                if not (last and u == 1):
                    silu_and_store(b, u, i, first)

        def silu_and_store(b, u, i, first):
            act.wait_ge(conv_done, b + 1)
            if not first:
                act.wait_ge(stored[u], i * 16)
            nc.scalar.activation(act_out[:, u], conv[:, :], ACT.Silu).then_inc(silu, 1)
            act.wait_ge(silu, b + 1)
            act.dma_start(xbcT[ds(b * P, P), :], act_out[:, u]).then_inc(stored[u], 16)

        def dt_split():
            act.wait_ge(dt_in, 16)
            nc.scalar.activation(wdt["hi"], wdt_raw[:, :, :], ACT.Copy).then_inc(dt_hi, 1)

        def decays():
            nc.scalar.activation(ea[:, :], K["alog"][:, :], ACT.Exp).then_inc(act_dt, 1)
            act.wait_ge(dve_dt, 3)
            nc.scalar.activation(t2[:, :, :], t2[:, :, :], ACT.Exp, scale=-1.0).then_inc(act_dt, 1)
            act.wait_ge(dve_dt, 4)
            nc.scalar.activation(t4[:, :, :], t3[:, :, :], ACT.Ln).then_inc(act_dt, 1)

        def finish():
            silu_and_store(NB_XBC - 1, 1, NP_ - 1, False)
            act.wait_ge(dve_dt, 18)
            nc.scalar.activation(S["eacs"][:, :, :], t1[:, :, :], ACT.Exp).then_inc(act_dt, 1)
            nc.scalar.activation(S["cdec"][:, :, :], ps_sum[:, 1, 0:NT * SSM_H].rearrange("p (t h) -> p t h", h=SSM_H), ACT.Exp).then_inc(act_dt, 1)
            nc.scalar.activation(t2[:, :, :], t2[:, :, :], ACT.Exp).then_inc(act_dt, 1)

        def at_half():
            dt_split()
            split(0, 0)

        nm["scalar"](act, at_half)
        split(1, 1)
        act.wait_ge(const["made"], 3)
        nc.scalar.activation(mem["ones"][:, :], K["ones"][:, :], ACT.Copy)
        nc.scalar.activation(mem["tri"][:, :], K["tri"][:, :], ACT.Copy)
        const["scalar_waves"](act)
        body(0, True, False)
        decays()
        with act.Fori(1, NP_ - 1) as i:
            body(i, False, False)
        body(NP_ - 1, False, True)
        return finish

    def gpsimd(pool):
        const["gpsimd"](pool)
        nm["gpsimd"](pool)

    def vector(dve):
        c = Chain(dve, conv_step, 2 * SSM_CONV - 2)

        def split(b, u):
            dve.wait_ge(w_hi, b + 1)
            nc.vector.tensor_tensor(w["lo"][:, 1, :, u * P:(u + 1) * P], raw[:, u], w["hi"][:, 1, :, u * P:(u + 1) * P].bitcast(F32), ALU.subtract).then_inc(w_lo, 1)

        def body(i, first, last):
            c.turn(i)
            for u in range(2):
                b = i * 2 + u
                tap = lambda j: K["pc1"][:, ds(b + PC_CW + j * NB_XBC, 1)]
                dve.wait_ge(evac, b + 1)
                if not (first and u == 0):
                    dve.wait_ge(silu, b)
                c.link(nc.vector.tensor_scalar(conv[:, :], pre[:, SSM_CONV - 1:], tap(SSM_CONV - 1), K["pc1"][:, ds(b + PC_CB, 1)], ALU.mult, ALU.add))
                for j in range(SSM_CONV - 2, -1, -1):
                    ins = nc.vector.scalar_tensor_tensor(conv[:, :], pre[:, j:j + L], tap(j), conv[:, :], ALU.mult, ALU.add)
                    if j:
                        c.link(ins)
                    else:
                        ins.then_inc(conv_done, 1)
                if not last:
                    split(b + 2, u)
                else:
                    kv["vector"](dve, u)
            c.close()

        d = Chain(dve, dve_dt)

        def copy_dt():
            dve.wait_ge(dt_mm, 1)
            nc.vector.tensor_copy(dtT[:, :], ps_dtT.rearrange("p a b -> p (a b)")).then_inc(dt_copied, 1)

        def decays():
            dve.wait_ge(dt_turned, 1)
            d.link(nc.vector.tensor_tensor(t1[:, :, :], ps_dt[:, :, 0], repeat(K["dtb"][:, :], NT), ALU.add))
            d.link(nc.vector.tensor_tensor(t1[:, :, :], ps_dt[:, :, 1], t1[:, :, :], ALU.add))
            d.link(nc.vector.scalar_tensor_tensor(t2[:, :, :], t1[:, :, :], -1.0, t1[:, :, :], ALU.mult, ALU.max))
            dve.wait_ge(act_dt, 2)
            d.link(nc.vector.tensor_scalar(t3[:, :, :], t2[:, :, :], 1.0, None, ALU.add))
            dve.wait_ge(act_dt, 3)
            d.link(nc.vector.tensor_scalar(t3[:, :, :], t3[:, :, :], 1.0, None, ALU.subtract))
            d.link(nc.vector.tensor_scalar(S["dt"][:, :, :], t3[:, :, :], 0.0, None, ALU.is_equal))
            d.link(nc.vector.tensor_tensor(t3[:, :, :], t3[:, :, :], S["dt"][:, :, :], ALU.add))
            d.link(nc.vector.tensor_tensor(t4[:, :, :], t4[:, :, :], S["dt"][:, :, :], ALU.add))
            d.link(nc.vector.reciprocal(t3[:, :, :], t3[:, :, :]))
            d.link(nc.vector.tensor_tensor(t4[:, :, :], t4[:, :, :], t3[:, :, :], ALU.mult))
            d.link(nc.vector.tensor_tensor(t4[:, :, :], t4[:, :, :], t2[:, :, :], ALU.mult))
            d.link(nc.vector.scalar_tensor_tensor(S["dt"][:, :, :], t1[:, :, :], 0.0, t4[:, :, :], ALU.max, ALU.add))
            d.link(nc.vector.tensor_tensor(t1[:, :, :], S["dt"][:, :, :], repeat(ea[:, :], NT), ALU.mult))
            d.link(nc.vector.tensor_scalar(S["dA"][:, :, :], t1[:, :, :], -1.0, None, ALU.mult))
            d.link(nc.vector.tensor_copy(dA["hi"][:, :, :], S["dA"][:, :, :]))
            nc.vector.tensor_tensor(dA["lo"][:, :, :], S["dA"][:, :, :], dA["hi"][:, :, :].bitcast(F32), ALU.subtract).then_inc(da_ready, 1)

        def decay_sums():
            dve.wait_ge(sums, 1)
            acs = ps_sum[:, 0, 0:NT * SSM_H].rearrange("p (t h) -> p t h", h=SSM_H)
            tot = ps_sum[:, 1, 0:NT * SSM_H].rearrange("p (t h) -> p t h", h=SSM_H)
            d.link(nc.vector.tensor_copy(t1[:, :, :], acs))
            nc.vector.tensor_scalar(S["nacs"][:, :, :], t1[:, :, :], -1.0, None, ALU.mult)
            d.link(nc.vector.tensor_tensor(t2[:, :, :], tot, t1[:, :, :], ALU.subtract))
            d.link(nc.vector.memset(t3[:, 0, 0:1], 0.0))
            dve.wait_ge(act_dt, 6)
            nc.vector.tensor_tensor(S["wend"][:, :, :], t2[:, :, :], S["dt"][:, :, :], ALU.mult).then_inc(decays_made, 1)

        def at_half():
            dve.wait_ge(dt_hi, 1)
            nc.vector.tensor_tensor(wdt["lo"], wdt_raw[:, :, :], wdt["hi"].bitcast(F32), ALU.subtract).then_inc(dt_lo, 1)
            split(0, 0)

        const["vector"](dve)
        nm["vector"](dve, at_half)
        nc.vector.memset(pre[:, 0:SSM_CONV - 1], 0.0).then_inc(padded, 1)
        split(1, 1)
        const["vector_waves"](dve)
        copy_dt()
        body(0, True, False)
        decays()
        with dve.Fori(1, NP_ - 1) as i:
            body(i, False, False)
        body(NP_ - 1, False, True)
        decay_sums()

    def tensor(pe):
        def project_half(u, half, ks=range(NK)):
            for k in ks:
                ins = product(nc, ps[:, u, half], {p: w[p][:, 1, k, u * P:(u + 1) * P] for p in w},
                              {p: hT[p][:, k, half * HALF:(half + 1) * HALF] for p in w}, k == 0, k == NK - 1)
            return ins

        def body(i, first, last):
            for u in range(2):
                b = i * 2 + u
                if first and u == 0:
                    continue
                pe.wait_ge(w_lo, b + 1)
                if not first:
                    pe.wait_ge(evac, b - 1)
                project_half(u, 0)
                project_half(u, 1).then_inc(mm, 1)

        const["tensor"](pe)
        for t in range(NT):
            nm["tensor"](pe, t)
            if t == NT - 3:
                pe.wait_ge(w_lo, 1)
                pe.wait_ge(nm["lo_done"], NT // 2)
                project_half(0, 0, range(NK // 2))
            if t == NT - 2:
                project_half(0, 0, range(NK // 2, NK))
        pe.wait_ge(dt_lo, 1)
        pe.wait_ge(nm["gained"], NT - 1)
        for half in range(2):
            pe.wait_ge(nm["lo_done"], (half + 1) * NT // 2)
            for k in range(NK):
                for part in ("hi", "lo"):
                    ins = nc.tensor.matmul(ps_dtT[:, half], wdt_both[:, k].rearrange("p a b -> p (a b)"), hT[part][:, k, half * HALF:(half + 1) * HALF],
                                           start=k == 0 and part == "hi", stop=k == NK - 1 and part == "lo")
        ins.then_inc(dt_mm, 1)
        project_half(0, 1).then_inc(mm, 1)
        pe.wait_ge(dt_copied, 1)
        for t in range(NT):
            ins = nc.tensor.transpose(ps_dt[:, t].rearrange("p a b -> p (a b)"), dtT[:, t * P:(t + 1) * P], K["ident"][0:2 * SSM_H, 0:2 * SSM_H])
        ins.then_inc(dt_turned, 1)
        body(0, True, False)
        with pe.Fori(1, NP_ - 1) as i:
            body(i, False, False)
        body(NP_ - 1, False, True)
        pe.wait_ge(da_ready, 1)
        for n, m in enumerate(("tri", "ones")):
            for part in ("hi", "lo"):
                ins = nc.tensor.matmul(ps_sum[:, n, 0:NT * SSM_H], mem[m][:, :], dA[part][:, :, :].rearrange("p t h -> p (t h)"),
                                       start=part == "hi", stop=part == "lo")
        ins.then_inc(sums, 1)

    return {"sync": sync, "scalar": scalar, "gpsimd": gpsimd, "vector": vector, "tensor": tensor,
            "stored": stored, "da_ready": da_ready, "decays_made": decays_made, "mm": mm}


def scan(nc, r, a, K, hT, xbcT, S, proj, y_out, mem, xbc_stored, xbc_mm, da_ready, decays_made):
    w_in = a["w_in"].rearrange("o (k p) c -> p (o k) c", p=P)
    proj_v = proj.rearrange("(t p) c -> p t c", p=P)
    xbc_v = xbcT.rearrange("(b p) l -> p b l", p=P)
    NX = SSM_W // P
    HS = 4
    NS = SSM_H // HS
    raw, w, stage, xc, spread_dA, W, off, y, state = (mem[n] for n in ("raw", "w", "stage", "xc", "spread_dA", "W", "off", "y", "state"))
    xt, xdt, xw, xd = mem["x4"]
    bt = r.sb("bt", [P, SSM_G, P])
    ps, ps_x, ps_bc, ps_s, ps_y = (mem[n] for n in ("ps", "ps_x", "ps_bc", "ps_s", "ps_y"))
    raw_in, w_hi, w_lo = r.sem("raw_in"), r.sem("w_hi"), r.sem("w_lo")
    unit_mm, unit_evac = r.sem("unit_mm"), r.sem("unit_evac")
    stored = [r.sem(f"stored{u}") for u in range(2)]
    y_stored = [r.sem(f"y_stored{u}") for u in range(2)]
    xc_in = [r.sem(f"xc_in{u}") for u in range(2)]
    x_turned, bc_mm, x_copied, bt_copied = r.sem("x_turned"), r.sem("bc_mm"), r.sem("x_copied"), r.sem("bt_copied")
    dA_spread, decay_mm, seg_done, exp_done = r.sem("dA_spread"), r.sem("decay_mm"), r.sem("seg_done"), r.sem("exp_done")
    W_done, xdt_done, xw_done, xd_done = r.sem("W_done"), r.sem("xdt_done"), r.sem("xw_done"), r.sem("xd_done")
    off_mm, off_scaled, off_skip = r.sem("off_mm"), r.sem("off_scaled"), r.sem("off_skip")
    y_mm, y_done, state_mm, state_faded, state_done = r.sem("y_mm"), r.sem("y_done"), r.sem("state_mm"), r.sem("state_faded"), r.sem("state_done")
    decays = [ps_s[:, :, :], ps_y[:, 0:HPG, :].rearrange("p (h c) q -> p h (c q)", c=2),
              ps_y[:, HPG:, :].rearrange("p (h c) q -> p h (c q)", c=2), ps_s[:, :, :]]
    NJ = NT // 2
    NU = NT // 2
    kv_at = lambda n: KV0 + n * PB

    def scalars(name, t, n=SSM_P):
        return S[name][:, ds(t, 1), :].rearrange("p o h -> p (o h)").unsqueeze(2).to_broadcast([P, SSM_H, n])

    def turns(eng, body):
        body(0, True)
        with eng.Fori(1, NJ) as j:
            body(j, False)

    def weights(sp, n, first, col):
        if not first:
            sp.wait_ge(w_hi, n)
            sp.wait_ge(w_lo, n)
        sp.dma_start(raw[:, :, :], w_in[:, :, ds(col, PB)]).then_inc(raw_in, 16)

    def first_weights(sp, _):
        weights(sp, 0, True, kv_at(0))

    def sync(sp):
        def tile(j, u, first):
            if not first:
                sp.wait_ge(off_mm, j * 2 + u - 1)
            sp.dma_start(xc[:, u], xbc_v[:, :, ds((j * 2 + u) * P, P)]).then_inc(xc_in[u], 16)

        def body(j, first):
            tile(j, 0, first)
            weights(sp, j * 2 + 2, False, j * PB + Z0)
            tile(j, 1, first)
            weights(sp, j * 2 + 3, False, j * PB + Q0)

        weights(sp, 1, False, kv_at(1))
        for u in range(2):
            sp.wait_ge(xbc_stored[u], 16 * NB_XBC // 2)
        turns(sp, body)

    def split_hi(act, n, u):
        act.wait_ge(raw_in, n * 16 + 16)
        nc.scalar.activation(w["hi"][:, u], raw[:, :, :], ACT.Copy).then_inc(w_hi, 1)

    def split_lo(dve, n, u):
        dve.wait_ge(w_hi, n + 1)
        nc.vector.tensor_tensor(w["lo"][:, u], raw[:, :, :], w["hi"][:, u].bitcast(F32), ALU.subtract).then_inc(w_lo, 1)

    def first_hi(act, n):
        if n == 1:
            act.wait_ge(xbc_mm, NB_XBC)
        split_hi(act, n, n)

    def first_lo(dve, n):
        if n == 1:
            dve.wait_ge(xbc_mm, NB_XBC)
        split_lo(dve, n, n)

    def scalar(act, xbc_end):
        def split(n, u):
            act.wait_ge(unit_mm, (n - 1) * NU)
            split_hi(act, n, u)

        def evacuate(n, u, func, col, stored_before, between=None):
            if stored_before is not None:
                act.wait_ge(stored[u], stored_before)
            for m in range(NU):
                act.wait_ge(unit_mm, n * NU + m + 1)
                nc.scalar.activation(stage[:, u, 2 * m:2 * m + 2, :], ps[:, m % 2], func).then_inc(unit_evac, 1)
                if between and m == 1:
                    between()
            act.wait_ge(unit_evac, n * NU + NU)
            act.dma_start(proj_v[:, :, ds(col, PB)], stage[:, u]).then_inc(stored[u], 16)

        def tile(t, first):
            act.wait_ge(bc_mm, t + 1)
            if not first:
                act.wait_ge(state_mm, t)
            nc.scalar.activation(bt[:, :, :], ps_bc[:, 0], ACT.Copy).then_inc(bt_copied, 1)
            act.wait_ge(x_turned, t + 1)
            if not first:
                act.wait_ge(xd_done, t)
            nc.scalar.activation(xt[:, :, :], ps_x[:, :, :], ACT.Copy).then_inc(x_copied, 1)
            for s in range(NS):
                act.wait_ge(seg_done, t * NS + s + 1)
                grp = W[:, HS * s:HS * (s + 1), :]
                nc.scalar.activation(grp, grp, ACT.Exp).then_inc(exp_done, 1)

        def body(j, first, last):
            tile(j * 2, first)
            split(j * 2 + 3, 1)
            evacuate(j * 2 + 2, 0, ACT.Silu, j * PB, j * 16 + 16)
            tile(j * 2 + 1, False)
            if not last:
                split(j * 2 + 4, 0)
            evacuate(j * 2 + 3, 1, ACT.Copy, j * PB + SSM_W, j * 16 + 16)

        evacuate(0, 0, ACT.Copy, SSM_W + Q_H * HD, None, xbc_end)
        split(2, 0)
        evacuate(1, 1, ACT.Copy, SSM_W + Q_H * HD + PB, None)
        body(0, True, False)
        with act.Fori(1, NJ - 1) as j:
            body(j, False, False)
        body(NJ - 1, False, True)
        for u in range(2):
            act.wait_ge(stored[u], 16 * (NJ + 1))

    def gpsimd(pool):
        def spread_tile(t, first):
            for s in range(NS):
                if not first:
                    pool.wait_ge(decay_mm, t * NS - (NS - 1 - s))
                for part in ("hi", "lo"):
                    heads = mem["dA"][part][:, ds(t, 1), HS * s:HS * (s + 1)].bitcast(F32).rearrange("p o h -> p (o h)")
                    nc.gpsimd.tensor_tensor(spread_dA[part][:, s], repeat(K["tri"][:, :], HS), spread(heads, P), ALU.mult).then_inc(dA_spread, 1)

        def tile(t, u, first, last):
            pool.wait_ge(x_copied, t + 1)
            if first:
                pool.wait_ge(decays_made, 1)
            else:
                pool.wait_ge(y_mm, t)
                pool.wait_ge(state_mm, t)
                pool.wait_ge(off_skip, t)
            nc.gpsimd.tensor_tensor(xdt[:, :, :], xt[:, :, :], scalars("dt", t), ALU.mult).then_inc(xdt_done, 1)
            nc.gpsimd.tensor_tensor(xw[:, :, :], xt[:, :, :], scalars("wend", t), ALU.mult).then_inc(xw_done, 1)
            nc.gpsimd.tensor_tensor(xd[:, :, :], xt[:, :, :], spread(K["dskip"][:, :], SSM_P), ALU.mult).then_inc(xd_done, 1)
            if not last:
                spread_tile(t + 1, False)
            pool.wait_ge(xd_done, t + 1)
            pool.wait_ge(off_scaled, t + 1)
            nc.gpsimd.tensor_tensor(off[:, :, :], off[:, :, :], xd[:, :, :], ALU.add).then_inc(off_skip, 1)
            pool.wait_ge(y_done, t + 1)
            pool.dma_start(y_out[ds(t * P, P), :], y[:, u].rearrange("p h q -> p (h q)")).then_inc(y_stored[u], 16)

        def body(j, first, last):
            for u in range(2):
                tile(j * 2 + u, u, first and u == 0, last and u == 1)

        pool.wait_ge(da_ready, 1)
        spread_tile(0, True)
        body(0, True, False)
        with pool.Fori(1, NJ - 1) as j:
            body(j, False, False)
        body(NJ - 1, False, True)
        for u in range(2):
            pool.wait_ge(y_stored[u], 16 * NJ)

    def vector(dve):
        def split(n, u):
            dve.wait_ge(unit_mm, (n - 1) * NU)
            split_lo(dve, n, u)

        def before(t, first):
            for s in range(NS):
                dve.wait_ge(decay_mm, t * NS + s + 1)
                if not first and s == 0:
                    dve.wait_ge(y_mm, t)
                for h in range(HS):
                    head = HS * s + h
                    ins = nc.vector.scalar_tensor_tensor(W[:, head, :], decays[s][:, h, :], S["nacs"][:, ds(t, 1), head],
                                                         K["cap"][:, :], ALU.add, ALU.min)
                ins.then_inc(seg_done, 1)
            for g in range(SSM_G):
                dve.wait_ge(exp_done, t * NS + (g + 1) * NS // SSM_G)
                heads = W[:, HPG * g:HPG * (g + 1), :]
                nc.vector.tensor_tensor(heads, heads, repeat(ps_bc[:, 1, g, :], HPG), ALU.mult).then_inc(W_done, 1)

        def after(t, u, first, y_before):
            dve.wait_ge(off_mm, t + 1)
            if not first:
                dve.wait_ge(y_done, t)
            nc.vector.tensor_tensor(off[:, :, :], ps_x[:, :, :], scalars("eacs", t), ALU.mult).then_inc(off_scaled, 1)
            if not first:
                dve.wait_ge(state_done, t)
            nc.vector.tensor_tensor(state[:, :, :], state[:, :, :], scalars("cdec", t), ALU.mult).then_inc(state_faded, 1)
            dve.wait_ge(y_mm, t + 1)
            dve.wait_ge(off_skip, t + 1)
            if y_before is not None:
                dve.wait_ge(y_stored[u], y_before)
            nc.vector.tensor_tensor(y[:, u], ps_y[:, :, :], off[:, :, :], ALU.add).then_inc(y_done, 1)
            dve.wait_ge(state_mm, t + 1)
            dve.wait_ge(state_faded, t + 2)
            nc.vector.tensor_tensor(state[:, :, :], ps_x[:, :, :], state[:, :, :], ALU.add).then_inc(state_done, 1)

        def body(j, first, last):
            for u in range(2):
                t = j * 2 + u
                before(t, first and u == 0)
                if not (last and u == 1):
                    split(j * 2 + 3 + u, 1 - u)
                after(t, u, first and u == 0, None if first else j * 16)

        dve.wait_ge(decays_made, 1)
        nc.vector.memset(state[:, :, :], 0.0).then_inc(state_faded, 1)
        split(2, 0)
        dve.wait_ge(state_faded, 1)
        body(0, True, False)
        with dve.Fori(1, NJ - 1) as j:
            body(j, False, False)
        body(NJ - 1, False, True)

    def tensor(pe):
        def project(n, u, first=False):
            pe.wait_ge(w_lo, n + 1)
            for t in range(NT):
                m = t // 2
                if t % 2 == 0 and not (first and m < 2):
                    pe.wait_ge(unit_evac, n * NU + m - 1)
                for k in range(NK):
                    ins = product(nc, ps[:, m % 2, t % 2, :], {p: hT[p][:, k, t * P:(t + 1) * P] for p in w},
                                  {p: w[p][:, u, k, :] for p in w}, k == 0, k == NK - 1)
                if t % 2:
                    ins.then_inc(unit_mm, 1)

        def before(t, u, first, xc_full):
            def decay(s):
                pe.wait_ge(dA_spread, (t * NS + s + 1) * 2)
                if s == 0 and not first:
                    pe.wait_ge(seg_done, t * NS)
                if s == 1 and not first:
                    pe.wait_ge(y_done, t)
                if s == 3:
                    pe.wait_ge(seg_done, t * NS + 1)
                nc.tensor.matmul(decays[s], mem["ones"][:, :], spread_dA["hi"][:, s], start=True, stop=False)
                nc.tensor.matmul(decays[s], mem["ones"][:, :], spread_dA["lo"][:, s], start=False, stop=True).then_inc(decay_mm, 1)

            pe.wait_ge(xc_in[u], xc_full)
            if not first:
                pe.wait_ge(W_done, t * SSM_G)
            for g in range(SSM_G):
                nc.tensor.transpose(ps_bc[:, 0, g, :], xc[:, u, NX + g, :], K["ident"][:, :])
                ins = nc.tensor.matmul(ps_bc[:, 1, g, :], xc[:, u, NX + g, :], xc[:, u, NX + SSM_G + g, :], start=True, stop=True)
            ins.then_inc(bc_mm, 1)
            decay(0)
            if not first:
                pe.wait_ge(state_done, t)
            for b in range(NX):
                ins = nc.tensor.transpose(ps_x[:, 2 * b:2 * b + 2, :].rearrange("p a b -> p (a b)"), xc[:, u, b, :], K["ident"][:, :])
            ins.then_inc(x_turned, 1)
            for s in range(1, NS):
                decay(s)

        def after(t, u, first):
            pe.wait_ge(x_copied, t + 1)
            if not first:
                pe.wait_ge(state_done, t)
            for g in range(SSM_G):
                ins = nc.tensor.matmul(ps_x[:, HPG * g:HPG * (g + 1), :], xc[:, u, NX + SSM_G + g, :], state[:, HPG * g:HPG * (g + 1), :],
                                       start=True, stop=True)
            ins.then_inc(off_mm, 1)
            pe.wait_ge(xdt_done, t + 1)
            pe.wait_ge(seg_done, t * NS + 3)
            for h in range(SSM_H):
                if h % HPG == 0:
                    pe.wait_ge(W_done, t * SSM_G + h // HPG + 1)
                ins = nc.tensor.matmul(ps_y[:, h, :], W[:, h, :], xdt[:, h, :], start=True, stop=True)
            ins.then_inc(y_mm, 1)
            pe.wait_ge(bt_copied, t + 1)
            pe.wait_ge(xw_done, t + 1)
            pe.wait_ge(off_scaled, t + 1)
            for g in range(SSM_G):
                ins = nc.tensor.matmul(ps_x[:, HPG * g:HPG * (g + 1), :], bt[:, g, :], xw[:, HPG * g:HPG * (g + 1), :], start=True, stop=True)
            ins.then_inc(state_mm, 1)

        def body(j, first):
            for u in range(2):
                t = j * 2 + u
                before(t, u, first and u == 0, j * 16 + 16)
                project(j * 2 + 2 + u, u)
                after(t, u, first and u == 0)

        project(0, 0, True)
        project(1, 1)
        pe.wait_ge(decays_made, 1)
        pe.wait_ge(state_faded, 1)
        turns(pe, body)

    return {"sync": sync, "scalar": scalar, "gpsimd": gpsimd, "vector": vector, "tensor": tensor,
            "first": {"sync": first_weights, "scalar": first_hi, "vector": first_lo}}


def scan_memory(r, rs):
    by_head = lambda ap: ap.rearrange("p (h q) -> p h q", q=SSM_P)
    flat = lambda ap: ap.rearrange("p a b -> p (a b)")
    mem = {"raw": r.sb("raw", [P, NK, PB])}
    mem["w"] = {part: r.sb(f"w_{part}", [P, 2, NK, PB], F32R) for part in ("hi", "lo")}
    mem["stage"] = r.sb("stage", [P, 2, NT, PB])
    mem["raw_xbc"] = mem["stage"][:, 0].rearrange("p t (a b) -> p (t a b)", b=P).rearrange("p (u k b) -> p u k b", u=2, b=P)
    shared = r.sb("shared", [P, NT * D])
    mem["x_sb"] = shared[:, :].rearrange("p (t d) -> p t d", d=D)
    XC, XW, W_ = 2 * NB_XBC * P, 2 * L, SSM_H * P
    mem["xc"] = shared[:, 0:XC].rearrange("p (u b l) -> p u b l", u=2, l=P)
    mem["act_out"] = shared[:, XC:XC + XW].rearrange("p (u l) -> p u l", u=2)
    mem["W"] = shared[:, XC + XW:XC + XW + W_].rearrange("p (h l) -> p h l", l=P)
    x2 = r.sb("x2", [P, 2, L])
    mem["x4"] = [by_head(x2[:, n]) for n in range(2)] + [by_head(mem["act_out"][:, n]) for n in range(2)]
    mem["full"] = x2[:, :, :].rearrange("p u (k l) -> p u k l", l=P)
    mem["spread_dA"] = {part: rs.sb(f"spread_{part}", [P, SSM_H // 4, 4, P], F32R) for part in ("hi", "lo")}
    mem["dA"] = {part: rs.sb(f"dA_{part}", [P, NT, SSM_H], F32R) for part in ("hi", "lo")}
    mem["ones"], mem["tri"] = rs.sb("ones", [P, P], F32R), rs.sb("tri", [P, P], F32R)
    off, y, state = r.sb("off", [P, SSM_H, SSM_P]), r.sb("y", [P, 2, SSM_H, SSM_P]), r.sb("state", [P, SSM_H, SSM_P])
    mem["off"], mem["junk"], mem["conv"] = off, flat(off[:, :, :]), flat(off[:, :, :])
    mem["y"], mem["xn"] = y, y[:, :].rearrange("p u h q -> p u (h q)")
    mem["pre"] = y[:, :].rearrange("p u h q -> p (u h q)")[:, 0:SSM_CONV - 1 + L]
    mem["state"], mem["dtT"] = state, flat(state[0:2 * SSM_H])
    mem["t4"] = [flat(state[:, :, :])[:, n * P:(n + 1) * P].rearrange("p (t h) -> p t h", h=SSM_H) for n in range(4)]
    ps_t = r.ps("ps_t", [P, NK, P])
    ps_xbc = r.ps("ps_xbc", [P, 2, 2, HALF])
    ps_5, ps_6 = r.ps("ps_5", [P, HALF]), r.ps("ps_6", [P, HALF])
    mem["ps_t"], mem["ps"] = ps_t[:, :, :], flat(ps_t[:, :, :]).rearrange("p (a b c) -> p a b c", a=2, c=PB)
    mem["ps_xbc"] = ps_xbc
    mem["ps_x"] = by_head(flat(ps_xbc[:, 0]))
    mem["ps_y"] = by_head(flat(ps_xbc[:, 1]))
    mem["ps_dt"] = ps_5[:, 0:2 * P].rearrange("p (t a h) -> p t a h", a=2, h=SSM_H)
    mem["ps_bc"] = ps_5[:, :].rearrange("p (a g l) -> p a g l", a=2, l=P)
    mem["ps_const"], mem["ps_sum"] = ps_6[:, :], ps_6[:, :].rearrange("p (a b) -> p a b", a=2)
    mem["ps_s"] = ps_6[:, :].rearrange("p (h l) -> p h l", l=P)
    return mem


def scan_stage(nc, a, K, hT, xbcT, S, proj, y_out):
    with ExitStack() as ctx:
        r, rs = Room(nc, ctx, "xbc"), Room(nc, ctx, "scan")
        mem = scan_memory(r, rs)
        first = {}
        x = xbc(nc, r, a, K, hT, xbcT, S, mem, first)
        sc = scan(nc, rs, a, K, hT, xbcT, S, proj, y_out, mem, x["stored"], x["mm"], x["da_ready"], x["decays_made"])
        first.update(sc["first"])
        with nc.Block() as block:

            @block.sync
            def _(sp):
                x["sync"](sp)
                sc["sync"](sp)

            @block.scalar
            def _(act):
                sc["scalar"](act, x["scalar"](act))

            @block.gpsimd
            def _(pool):
                x["gpsimd"](pool)
                sc["gpsimd"](pool)

            @block.vector
            def _(dve):
                x["vector"](dve)
                sc["vector"](dve)

            @block.tensor
            def _(pe):
                x["tensor"](pe)
                sc["tensor"](pe)
        r.clear(rs)


def mix_stage(nc, a, K, proj, y_in, x_new, rstd):
    w_out = a["w_out"].rearrange("o (m p) c -> p (o m) c", p=P)
    x = a["x"].rearrange("o t d -> (o t) d")
    NQB = Q_H * HD // P
    QKW = QK_H * HD
    ROWS = 2 * KV_H
    NW = 8
    WB = NM * 2 // NW
    with ExitStack() as ctx:
        r = Room(nc, ctx, "mix")
        with nc.sbuf_tensor("mix_w_raw", [P, NM, D], F32) as w_raw:
            pass
        w = {part: r.sb(f"w_{part}", [P, NM, D], F32R) for part in ("lo", "hi")}
        mix = {part: r.sb(f"mix_{part}", [P, NM, P], F32R) for part in ("hi", "lo")}
        qk, qn = r.sb("qk", [P, QK_H, HD]), r.sb("qn", [P, QK_H, HD])
        v_own, v_mixed = r.sb("v_own", [P, KV_W]), r.sb("v_mixed", [P, KV_W])
        yz, x_io = r.sb("yz", [P, 2, D]), r.sb("x_io", [P, D])
        kd = r.sb("kd", [P, KV_H, 2, HD])
        qT = r.sb("qT", [P, 2, NQB, CHUNK])
        kT = r.sb("kT", [P, KV_H, 3, CHUNK])
        prob, probT = r.sb("prob", [P, 2, ROWS, P]), r.sb("probT", [P, 2, ROWS, P])
        full = r.sb("full", [P, NK, P])
        rope = r.sb("rope", [P, 4, QK_H, RH])
        qk_ms, qk_rs = r.sb("qk_ms", [P, QK_H]), r.sb("qk_rs", [P, QK_H])
        y_ms, y_rs = r.sb("y_ms", [P, 1]), r.sb("y_rs", [P, 1])
        power, eps = r.sb("power", [P, QK_H]), r.sb("eps", [P, QK_H])
        top, ntop, sink_arg = (r.sb(n, [P, 2, ROWS]) for n in ("top", "ntop", "sink_arg"))
        sink_exp, row_sum, inv = (r.sb(n, [P, 2, ROWS]) for n in ("sink_exp", "row_sum", "inv"))
        ps_s = r.ps("ps_s", [P, ROWS, P])
        ps_t = r.ps("ps_t", [P, ROWS, P])
        ps_a = r.ps("ps_a", [P, NQB, 2, CHUNK])
        ps_o = r.ps("ps_o", [P, 2, HALF])
        w_in = [r.sem(f"w_in{n}") for n in range(NW)]
        w_hi, w_lo = r.sem("w_hi"), r.sem("w_lo")
        qk_in, z_in, y_in_, x_in = r.sem("qk_in"), r.sem("z_in"), r.sem("y_in"), r.sem("x_in")
        v_own_in, v_own2_in, v_before_in = r.sem("v_own_in"), r.sem("v_own2_in"), r.sem("v_before_in")
        x_out = r.sem("x_out")
        ssq = r.sb("ssq", [P, NT])
        x_squared, meaned, rstd_done = r.sem("x_squared"), r.sem("meaned"), r.sem("rstd_done")
        set_power = r.sem("set_power")
        qk_squared, qk_summed, qk_eps, qk_rs_ready = r.sem("qk_squared"), r.sem("qk_summed"), r.sem("qk_eps"), r.sem("qk_rs_ready")
        qk_step, qk_read, qn_done, kd_done = r.sem("qk_step"), r.sem("qk_read"), r.sem("qn_done"), r.sem("kd_done")
        q_turned, k_turned, qT_done, kT_moved, kT_done = (r.sem(n) for n in ("q_turned", "k_turned", "qT_done", "kT_moved", "kT_done"))
        s_mm, top_step, ntop_done, exp_done = r.sem("s_mm"), r.sem("top_step"), r.sem("ntop_done"), r.sem("exp_done")
        inv_step, prob_done, prob_turned, probT_done, pv_mm = (r.sem(n) for n in ("inv_step", "prob_done", "prob_turned", "probT_done", "pv_mm"))
        at_hi, at_lo = r.sem("at_hi"), r.sem("at_lo")
        gated, y_squared, y_eps, y_rs_ready, y_scaled = (r.sem(n) for n in ("gated", "y_squared", "y_eps", "y_rs_ready", "y_scaled"))
        y_turned, gained, y_hi, y_lo = (r.sem(n) for n in ("y_turned", "gained", "y_hi", "y_lo"))
        out_mm, out_added = r.sem("out_mm"), r.sem("out_added")
        yt, zt = yz[:, 0], yz[:, 1]

        def piece(n):
            half, part = n // (NW // 2), n // (NW // 4) % 2
            row = part * NK + n % (NW // 4) * WB
            return slice(row, row + WB), slice(half * HALF, (half + 1) * HALF)

        w_part = lambda which, n: w[which][:, piece(n)[0], piece(n)[1]]
        w_raw_part = lambda n: w_raw[:, piece(n)[0], piece(n)[1]]
        w_out_part = lambda n: w_out[:, piece(n)[0], piece(n)[1]]
        flat = lambda ap: ap.rearrange("p a b -> p (a b)")

        def tiles(eng, body):
            body(0, True, False)
            body(1, False, False)
            with eng.Fori(2, NT - 1) as t:
                body(t, False, False)
            body(NT - 1, False, True)

        PIECES = {(0, "u0"): [0], (0, "u1"): [1], (0, "late"): [2, 3], (0, "end"): [4, 5], (1, "begin"): [6], (1, "u1"): [7]}

        def split_at(t, place, split):
            if isinstance(t, int):
                for n in PIECES.get((t, place), []):
                    split(n)

        with nc.Block() as block:

            @block.sync
            def _(sp):
                qk_cols = slice(SSM_W, SSM_W + QKW)
                v_cols = slice(SSM_W + QKW, SSM_W + QKW + KV_W)

                def load_qk(t):
                    sp.dma_start(qk[:, :, :], proj[ds(t * P, P), qk_cols].rearrange("t (h d) -> t h d", d=HD)).then_inc(qk_in, 16)

                def load_yz(t):
                    sp.dma_start(yt, y_in[ds(t * P, P), :]).then_inc(y_in_, 16)
                    sp.dma_start(zt, proj[ds(t * P, P), 0:SSM_W]).then_inc(z_in, 16)

                def load_w(start, end):
                    for n in range(start, end):
                        sp.dma_start(w_raw_part(n), w_out_part(n)).then_inc(w_in[n], 16)

                def load_v(t, before):
                    sp.wait_ge(pv_mm, before * 2 + 2)
                    sp.dma_start(v_own[:, :], proj[ds(t * P, P), v_cols]).then_inc(v_own_in, 16)
                    sp.dma_start(v_mixed[0:CHUNK, :], proj[ds(t * P, CHUNK), v_cols]).then_inc(v_own2_in, 16)
                    sp.dma_start(v_mixed[CHUNK:, :], proj[ds(before * P + CHUNK, CHUNK), v_cols]).then_inc(v_before_in, 16)

                def store(t):
                    sp.wait_ge(x_squared, t + 1)
                    sp.dma_start(x_new[ds(t * P, P), :], x_io[:, :]).then_inc(x_out, 16)
                    sp.wait_ge(x_out, t * 16 + 16)

                def body(t, stores, loads_qk, loads):
                    if stores:
                        store(t - 2)
                        sp.dma_start(x_io[:, :], x[ds((t - 1) * P, P), :]).then_inc(x_in, 16)
                    if loads:
                        sp.wait_ge(y_turned, t + 1)
                        load_yz(t + 1)
                    if loads_qk:
                        sp.wait_ge(qk_read, t + 2)
                        load_qk(t + 2)
                    if loads:
                        load_v(t + 1, t)

                load_qk(0)
                load_yz(0)
                sp.dma_start(v_own[:, :], proj[0:P, v_cols]).then_inc(v_own_in, 16)
                sp.dma_start(v_mixed[0:CHUNK, :], proj[0:CHUNK, v_cols]).then_inc(v_own2_in, 16)
                load_w(0, 2)
                sp.wait_ge(qk_read, 1)
                load_qk(1)
                load_w(2, 4)
                sp.dma_start(x_io[:, :], x[0:P, :]).then_inc(x_in, 16)
                sp.wait_ge(y_turned, 1)
                load_yz(1)
                load_w(4, NW)
                load_v(1, 0)
                sp.wait_ge(qk_read, 2)
                load_qk(2)
                body(1, False, True, True)
                with sp.Fori(2, NT - 2) as t:
                    body(t, True, True, True)
                body(NT - 2, True, False, True)
                body(NT - 1, True, False, False)
                store(NT - 2)
                sp.dma_start(x_io[:, :], x[(NT - 1) * P:, :]).then_inc(x_in, 16)
                store(NT - 1)

            @block.scalar
            def _(act):
                def split(n):
                    act.wait_ge(w_in[n], 16)
                    nc.scalar.activation(w_part("hi", n), w_raw_part(n), ACT.Copy).then_inc(w_hi, 1)

                def square_qk(t):
                    act.wait_ge(qk_in, t * 16 + 16)
                    nc.scalar.activation(qn[:, :, :], qk[:, :, :], ACT.Square, scale=HD ** -0.5).then_inc(qk_squared, 1)

                def square_y(t):
                    act.wait_ge(gated, t + 1)
                    nc.scalar.activation(zt, yt, ACT.Square, scale=SSM_W ** -0.5, accum_out=y_ms[:, :]).then_inc(y_squared, 1)

                def exps(t, u, keys):
                    act.wait_ge(ntop_done, t * 2 + u + 1)
                    for n in range(ROWS):
                        nc.scalar.activation(prob[:, u, n, 0:keys], ps_s[:, n, 0:keys], ACT.Exp, bias=ntop[:, u, n:n + 1], scale=SCALE,
                                             accum_out=row_sum[:, u, n:n + 1])
                    nc.scalar.activation(sink_exp[:, u], sink_arg[:, u], ACT.Exp).then_inc(exp_done, 1)

                def copy_probT(t, u, keys):
                    act.wait_ge(prob_turned, t * 2 + u + 1)
                    nc.scalar.activation(probT[0:keys, u], ps_t[0:keys], ACT.Copy).then_inc(probT_done, 1)

                def square_out(t):
                    act.wait_ge(out_added, t * 2 + 2)
                    junk = flat(probT[:, 0])
                    nc.scalar.activation(junk, x_io[:, :], ACT.Square, scale=D ** -0.5, accum_out=ssq[:, ds(t, 1)]).then_inc(x_squared, 1)

                def body(t, first, last):
                    if not isinstance(t, int) or t >= 2:
                        square_out(t - 2)
                    act.wait_ge(q_turned, t + 1)
                    if not first:
                        act.wait_ge(s_mm, t * 2)
                    nc.scalar.activation(qT[:, :, :, :].rearrange("p u b c -> p b u c"), ps_t[:, :, :].rearrange("p b (u c) -> p b u c", u=2), ACT.Copy).then_inc(qT_done, 1)
                    if not last:
                        act.wait_ge(kd_done, t + 1)
                        square_qk(t + 1)
                    keys0 = CHUNK if first else P
                    split_at(t, "begin", split)
                    exps(t, 0, keys0)
                    split_at(t, "u0", split)
                    exps(t, 1, P)
                    copy_probT(t, 0, keys0)
                    split_at(t, "u1", split)
                    if not last:
                        square_y(t + 1)
                    copy_probT(t, 1, P)
                    split_at(t, "late", split)
                    act.wait_ge(gained, t + 1)
                    if not first:
                        act.wait_ge(out_mm, t * 2)
                    nc.scalar.activation(mix["hi"][:, 0:NK, :], full[:, :, :], ACT.Copy).then_inc(y_hi, 1)
                    act.wait_ge(pv_mm, t * 2 + 2)
                    nc.scalar.activation(mix["hi"][:, NK:, :], ps_a[:, :, :, :].rearrange("p a b c -> p a (b c)"), ACT.Copy).then_inc(at_hi, 1)
                    split_at(t, "end", split)

                square_qk(0)
                square_y(0)
                tiles(act, body)
                square_out(NT - 2)
                square_out(NT - 1)

            @block.gpsimd
            def _(pool):
                def prepare(t):
                    pool.wait_ge(qk_summed, t + 1)
                    nc.gpsimd.tensor_tensor(qk_rs[:, :], qk_ms[:, :], eps[:, :], ALU.add).then_inc(qk_eps, 1)
                    pool.wait_ge(qk_eps, t + 1)
                    nc.gpsimd.tensor_tensor(qk_rs[:, :], qk_rs[:, :], power[:, :], ALU.pow).then_inc(qk_rs_ready, 1)
                    pool.wait_ge(y_in_, t * 16 + 16)
                    pool.wait_ge(z_in, t * 16 + 16)
                    nc.gpsimd.tensor_tensor(yt, yt, zt, ALU.mult).then_inc(gated, 1)
                    pool.wait_ge(y_squared, t + 1)
                    nc.gpsimd.tensor_tensor(y_rs[:, :], y_ms[:, :], eps[:, 0:1], ALU.add).then_inc(y_eps, 1)
                    pool.wait_ge(y_eps, t + 1)
                    nc.gpsimd.tensor_tensor(y_rs[:, :], y_rs[:, :], power[:, 0:1], ALU.pow).then_inc(y_rs_ready, 1)

                nc.gpsimd.memset(eps[:, :], EPS).then_inc(set_power, 1)
                nc.gpsimd.memset(power[:, :], -0.5).then_inc(set_power, 1)
                pool.wait_ge(set_power, 2)
                prepare(0)
                with pool.Fori(1, NT) as t:
                    prepare(t)
                for n, cols in enumerate((slice(0, NT - 1), slice(NT - 1, NT))):
                    pool.wait_ge(x_squared, NT - 1 + n)
                    nc.gpsimd.tensor_tensor(rstd[:, cols], ssq[:, cols], eps[:, cols], ALU.add).then_inc(meaned, 1)
                    pool.wait_ge(meaned, n + 1)
                    nc.gpsimd.tensor_tensor(rstd[:, cols], rstd[:, cols], power[:, cols], ALU.pow).then_inc(rstd_done, 1)

            @block.vector
            def _(dve):
                qc = Chain(dve, qk_step, 2)
                tc = Chain(dve, top_step, 4)
                ic = Chain(dve, inv_step, 4)

                def split(n):
                    dve.wait_ge(w_hi, n + 1)
                    nc.vector.tensor_tensor(w_part("lo", n), w_raw_part(n), w_part("hi", n).bitcast(F32), ALU.subtract).then_inc(w_lo, 1)

                def sum_qk(t):
                    dve.wait_ge(qk_squared, t + 1)
                    nc.vector.tensor_reduce(qk_ms[:, :], qn[:, :, :], AX.X, ALU.add).then_inc(qk_summed, 1)

                def scale_qk(t):
                    qc.turn(t)
                    dve.wait_ge(qk_rs_ready, t + 1)
                    nc.vector.tensor_tensor(qn[:, :, :], qk[:, :, :], spread(qk_rs[:, :], HD), ALU.mult).then_inc(qk_read, 1)
                    dve.wait_ge(qk_read, t + 1)
                    nc.vector.tensor_tensor(qn[:, 0:Q_H, :], qn[:, 0:Q_H, :], repeat(K["gq"][:, :], Q_H), ALU.mult)
                    qc.link(nc.vector.tensor_tensor(qn[:, Q_H:, :], qn[:, Q_H:, :], repeat(K["gk"][:, :], KV_H), ALU.mult))

                def rotate_qk(t, first):
                    cos, sin = (repeat(K[n][:, ds(t, 1), :].rearrange("p o f -> p (o f)"), QK_H) for n in ("cos", "sin"))
                    x1, x2 = qn[:, :, 0:RH], qn[:, :, RH:ROPE]
                    for n, (src, wave) in enumerate(((x1, cos), (x2, sin), (x2, cos), (x1, sin))):
                        ins = nc.vector.tensor_tensor(rope[:, n], src, wave, ALU.mult)
                    qc.link(ins)
                    nc.vector.tensor_tensor(x1, rope[:, 0], rope[:, 1], ALU.subtract)
                    nc.vector.tensor_tensor(x2, rope[:, 2], rope[:, 3], ALU.add).then_inc(qn_done, 1)
                    qc.close()
                    dve.wait_ge(qn_done, t + 1)
                    if not first:
                        dve.wait_ge(k_turned, t)
                    k_heads = qn[:, Q_H:, :].unsqueeze(2).to_broadcast([P, KV_H, 2, HD])
                    nc.vector.tensor_copy(kd[:, :, :, :], k_heads).then_inc(kd_done, 1)

                def scale_y(t):
                    dve.wait_ge(y_rs_ready, t + 1)
                    nc.vector.tensor_scalar(yt, yt, y_rs[:, :], None, ALU.mult).then_inc(y_scaled, 1)

                def add_out(t, half):
                    if half == 0:
                        dve.wait_ge(x_in, t * 16 + 16)
                    dve.wait_ge(out_mm, t * 2 + half + 1)
                    part = x_io[:, half * HALF:(half + 1) * HALF]
                    nc.vector.tensor_tensor(part, ps_o[:, half], part, ALU.add).then_inc(out_added, 1)

                def tops(t, u, keys):
                    dve.wait_ge(s_mm, t * 2 + u + 1)
                    tc.link(nc.vector.tensor_reduce(top[:, u], ps_s[:, :, 0:keys], AX.X, ALU.max))
                    tc.link(nc.vector.scalar_tensor_tensor(ntop[:, u], top[:, u], -SCALE, flat(K["nsink"][:, :, :]), ALU.mult, ALU.min))
                    nc.vector.tensor_tensor(sink_arg[:, u], flat(K["sink"][:, :, :]), ntop[:, u], ALU.add).then_inc(ntop_done, 1)

                def probs(t, u, keys):
                    dve.wait_ge(exp_done, t * 2 + u + 1)
                    ic.link(nc.vector.tensor_tensor(inv[:, u], row_sum[:, u], sink_exp[:, u], ALU.add))
                    ic.link(nc.vector.reciprocal(inv[:, u], inv[:, u]))
                    p = prob[:, u, :, 0:keys]
                    nc.vector.tensor_tensor(p, p, spread(inv[:, u], keys), ALU.mult).then_inc(prob_done, 1)

                def body(t, first, last):
                    tc.turn(t), ic.turn(t)
                    if not first:
                        dve.wait_ge(s_mm, t * 2)
                        nc.vector.tensor_copy(kT[:, :, 2, :], kT[:, :, 1, :]).then_inc(kT_moved, 1)
                        dve.wait_ge(kT_moved, t)
                    dve.wait_ge(k_turned, t + 1)
                    nc.vector.tensor_copy(kT[:, :, 0:2, :], ps_a[:, 0:KV_H]).then_inc(kT_done, 1)
                    if not last:
                        sum_qk(t + 1)
                    dve.wait_ge(y_turned, t + 1)
                    nc.vector.tensor_tensor(full[:, :, :], ps_t[:, :, :], spread(K["pc1"][:, PC_SSM:PC_SSM + NK], P), ALU.mult).then_inc(gained, 1)
                    keys0 = CHUNK if first else P
                    split_at(t, "begin", split)
                    tops(t, 0, keys0)
                    split_at(t, "u0", split)
                    probs(t, 0, keys0)
                    tops(t, 1, P)
                    if not first:
                        add_out(t - 1, 0)
                    if not last:
                        scale_qk(t + 1)
                    probs(t, 1, P)
                    split_at(t, "u1", split)
                    if not last:
                        rotate_qk(t + 1, False)
                        scale_y(t + 1)
                    split_at(t, "late", split)
                    tc.close(), ic.close()
                    dve.wait_ge(y_hi, t + 1)
                    nc.vector.tensor_tensor(mix["lo"][:, 0:NK, :], full[:, :, :], mix["hi"][:, 0:NK, :].bitcast(F32), ALU.subtract).then_inc(y_lo, 1)
                    dve.wait_ge(at_hi, t + 1)
                    nc.vector.tensor_tensor(mix["lo"][:, NK:, :], ps_a[:, :, :, :].rearrange("p a b c -> p a (b c)"),
                                            mix["hi"][:, NK:, :].bitcast(F32), ALU.subtract).then_inc(at_lo, 1)
                    if not first:
                        add_out(t - 1, 1)
                    split_at(t, "end", split)

                sum_qk(0)
                scale_qk(0)
                rotate_qk(0, True)
                scale_y(0)
                tiles(dve, body)
                for half in range(2):
                    add_out(NT - 1, half)

            @block.tensor
            def _(pe):
                def project(t, half, part):
                    if half == 0:
                        pe.wait_ge(at_lo if part else y_lo, t + 1)
                    pe.wait_ge(w_lo, (half * 2 + part + 1) * NW // 4)
                    cols = slice(half * HALF, (half + 1) * HALF)
                    for n in range(NK):
                        m = part * NK + n
                        ins = product(nc, ps_o[:, half], {p: mix[p][:, m, :] for p in w}, {p: w[p][:, m, cols] for p in w},
                                      n == 0 and not part, n == NK - 1 and part == 1)
                    if part:
                        ins.then_inc(out_mm, 1)

                def scores(t, u, first):
                    if u == 0:
                        pe.wait_ge(qT_done, t + 1)
                        pe.wait_ge(kT_done, t + 1)
                        if not first:
                            pe.wait_ge(exp_done, t * 2)
                    else:
                        pe.wait_ge(exp_done, t * 2 + 1)
                    for c in range(2):
                        rows = slice(c * HD, (c + 1) * HD)
                        for j in range(KV_H):
                            if u:
                                keys = kT[rows, j, 0:2, :]
                            else:
                                keys = kT[rows, j, 0:1, :] if first else kT[rows, j, 0:3:2, :]
                            n = CHUNK if first and not u else P
                            ins = nc.tensor.matmul(ps_s[:, c * KV_H + j, 0:n], qT[rows, u, 2 * j:2 * j + 2, :].rearrange("p a b -> p (a b)"), keys, start=True, stop=True)
                    ins.then_inc(s_mm, 1)

                def turn_probs(t, u, first):
                    pe.wait_ge(prob_done, t * 2 + u + 1)
                    if u:
                        pe.wait_ge(probT_done, t * 2 + 1)
                    else:
                        pe.wait_ge(gained, t + 1)
                    n = CHUNK if first and not u else P
                    for m in range(ROWS):
                        ins = nc.tensor.transpose(ps_t[0:n, m, :], prob[:, u, m, 0:n], K["ident"][:, :])
                    ins.then_inc(prob_turned, 1)

                def values(t, u, first):
                    pe.wait_ge(probT_done, t * 2 + u + 1)
                    if u:
                        pe.wait_ge(v_own_in, t * 16 + 16)
                        v = v_own[:, :]
                    else:
                        pe.wait_ge(v_own2_in, t * 16 + 16)
                        if not first:
                            pe.wait_ge(v_before_in, t * 16)
                        v = v_mixed[0:CHUNK if first else P, :]
                    n = v.shape[0]
                    for c in range(2):
                        for j in range(KV_H):
                            ins = nc.tensor.matmul(ps_a[c * HD:(c + 1) * HD, 2 * j:2 * j + 2, u, :], v[:, j * HD:(j + 1) * HD],
                                                   probT[0:n, u, c * KV_H + j, :], start=True, stop=True)
                    ins.then_inc(pv_mm, 1)

                def body(t, first, last):
                    pe.wait_ge(qn_done, t + 1)
                    if not first:
                        pe.wait_ge(probT_done, t * 2)
                    for b in range(NQB):
                        ins = nc.tensor.transpose(ps_t[:, b, :], qn[:, 2 * b:2 * b + 2, :].rearrange("p a b -> p (a b)"), K["ident"][:, :])
                    ins.then_inc(q_turned, 1)
                    if not first:
                        project(t - 1, 0, 0)
                    pe.wait_ge(kd_done, t + 1)
                    if not first:
                        pe.wait_ge(at_lo, t)
                    for j in range(KV_H):
                        ins = nc.tensor.transpose(ps_a[:, j].rearrange("p a b -> p (a b)"), kd[:, j].rearrange("p a b -> p (a b)"), K["ident"][:, :])
                    ins.then_inc(k_turned, 1)
                    pe.wait_ge(y_scaled, t + 1)
                    pe.wait_ge(qT_done, t + 1)
                    for b in range(NK):
                        ins = nc.tensor.transpose(ps_t[:, b, :], yt[:, b * P:(b + 1) * P], K["ident"][:, :])
                    ins.then_inc(y_turned, 1)
                    scores(t, 0, first)
                    if not first:
                        project(t - 1, 0, 1)
                    scores(t, 1, first)
                    turn_probs(t, 0, first)
                    if not first:
                        project(t - 1, 1, 0)
                    values(t, 0, first)
                    turn_probs(t, 1, first)
                    if not first:
                        project(t - 1, 1, 1)
                    values(t, 1, first)

                tiles(pe, body)
                project(NT - 1, 0, 0)
                project(NT - 1, 0, 1)
                pe.wait_ge(out_added, (NT - 1) * 2)
                project(NT - 1, 1, 0)
                project(NT - 1, 1, 1)


def ffn_stage(nc, a, K, hT, x_sb, src, rstd, out):
    w_in = a["w_ffn_in"].rearrange("o (k p) c -> p (o k) c", p=P)
    w_down = a["w_ffn_out"].rearrange("o (f p) c -> p (o f) c", p=P)
    LEAD = FFN_CONV - 1
    NPART = 2 * GF
    NOUT = 2 * NT
    with ExitStack() as ctx:
        r = Room(nc, ctx, "ffn")
        raw = r.sb("raw", [P, 2, NK, P])
        w = {part: r.sb(f"w_{part}", [P, NPART, NK, P], F32R) for part in ("hi", "lo")}
        down_raw = r.sb("down_raw", [P, GF, D])
        down = {part: r.sb(f"down_{part}", [P, GF, D], F32R) for part in ("hi", "lo")}
        pre = r.sb("pre", [P, LEAD + L])
        conv = r.sb("conv", [P, L])
        hid = {part: r.sb(f"hid_{part}", [P, GF, L], F32R) for part in ("hi", "lo")}
        ps_in = r.ps("ps_in", [P, 2, 2, HALF])
        ps_out = r.ps("ps_out", [P, 4, HALF])
        full = r.sb("full", [P, 2, NK, P])
        nm = norm(nc, r, src, PC_FFN, K, x_sb, hT, [ps_out[:, 2 * u:2 * u + 2, :].rearrange("p a (b c) -> p (a b) c", c=P) for u in range(2)],
                  [down_raw[:, 0], down_raw[:, 1]], [full[:, 0], full[:, 1]], rstd=rstd)
        raw_in = [r.sem(f"raw_in{u}") for u in range(2)]
        down_in, padded = r.sem("down_in"), r.sem("padded")
        w_hi, w_lo, down_hi, down_lo = r.sem("w_hi"), r.sem("w_lo"), r.sem("down_hi"), r.sem("down_lo")
        in_mm, evac, conv_step, conv_done, silu = r.sem("in_mm"), r.sem("evac"), r.sem("conv_step"), r.sem("conv_done"), r.sem("silu")
        hid_done, hid_hi, hid_lo = r.sem("hid_done"), r.sem("hid_hi"), r.sem("hid_lo")
        out_mm, added, x_out = r.sem("out_mm"), r.sem("added"), r.sem("x_out")

        def groups(eng, body):
            body(0, True, False)
            with eng.Fori(1, NG - 1) as g:
                body(g, False, False)
            body(NG - 1, False, True)

        with nc.Block() as block:

            @block.sync
            def _(sp):
                def body(g, first, last):
                    for q in range(NPART):
                        if not (first and q < 2):
                            sp.wait_ge(w_hi, g * NPART + q - 1)
                            sp.wait_ge(w_lo, g * NPART + q - 1)
                        col = g * (GF * P) + (q // 2) * P + (q % 2) * D_FF
                        sp.dma_start(raw[:, q % 2], w_in[:, :, ds(col, P)]).then_inc(raw_in[q % 2], 16)
                        if q == 1:
                            if not first:
                                sp.wait_ge(down_lo, g)
                            else:
                                sp.wait_ge(nm["turned"], NT)
                            sp.dma_start(down_raw[:, :, :], w_down[:, ds(g * GF, GF), :]).then_inc(down_in, 16)

                groups(sp, body)
                for t in range(NT):
                    sp.wait_ge(added, (NG - 1) * NOUT + 2 * t + 2)
                    sp.dma_start(out[t * P:(t + 1) * P, :], x_sb[:, t, :]).then_inc(x_out, 16)
                sp.wait_ge(x_out, 16 * NT)

            @block.scalar
            def _(act):
                for t in range(NT):
                    nm["load"](act, t)

                def split(g, q, first):
                    act.wait_ge(raw_in[q % 2], g * 32 + 16 * (q // 2) + 16)
                    if not first:
                        act.wait_ge(in_mm, (g - 1) * NPART + q + 1)
                    nc.scalar.activation(w["hi"][:, q], raw[:, q % 2], ACT.Copy).then_inc(w_hi, 1)

                def body(g, first, last):
                    for c in range(GF):
                        if c == 0:
                            split(g, 2, first)
                            split(g, 3, first)
                        act.wait_ge(in_mm, g * NPART + 2 * c + 1)
                        if first and c == 0:
                            act.wait_ge(padded, 1)
                        else:
                            act.wait_ge(conv_done, g * GF + c)
                        nc.scalar.activation(pre[:, LEAD:], ps_in[:, 0].rearrange("p a b -> p (a b)"), ACT.Copy).then_inc(evac, 1)
                        if c == 1:
                            act.wait_ge(down_in, g * 16 + 16)
                            if not first:
                                act.wait_ge(out_mm, g * NOUT)
                            nc.scalar.activation(down["hi"][:, :, :], down_raw[:, :, :], ACT.Copy).then_inc(down_hi, 1)
                        act.wait_ge(conv_done, g * GF + c + 1)
                        nc.scalar.activation(conv[:, :], conv[:, :], ACT.Silu).then_inc(silu, 1)
                        if c == 1 and not last:
                            split(g + 1, 0, False)
                            split(g + 1, 1, False)
                        act.wait_ge(hid_done, g * GF + c + 1)
                        if not first:
                            act.wait_ge(out_mm, g * NOUT)
                        nc.scalar.activation(hid["hi"][:, c], conv[:, :], ACT.Copy).then_inc(hid_hi, 1)

                nm["scalar"](act, lambda: (split(0, 0, True), split(0, 1, True)))
                groups(act, body)

            @block.vector
            def _(dve):
                cc = Chain(dve, conv_step, GF * (FFN_CONV - 1))

                def split(g, q, first):
                    dve.wait_ge(w_hi, g * NPART + q + 1)
                    nc.vector.tensor_tensor(w["lo"][:, q], raw[:, q % 2], w["hi"][:, q].bitcast(F32), ALU.subtract).then_inc(w_lo, 1)

                def add(g, n):
                    dve.wait_ge(out_mm, g * NOUT + n + 1)
                    part = x_sb[:, n // 2, (n % 2) * HALF:(n % 2 + 1) * HALF]
                    nc.vector.tensor_tensor(part, ps_out[:, n % 4], part, ALU.add).then_inc(added, 1)

                def body(g, first, last):
                    cc.turn(g)
                    for c in range(GF):
                        if c == 0:
                            split(g, 2, first)
                            split(g, 3, first)
                        f = g * GF + c
                        tap = lambda j: K["pc2"][:, ds(f + j * NF, 1)]
                        dve.wait_ge(evac, f + 1)
                        if not (first and c == 0):
                            dve.wait_ge(hid_hi, f)
                            dve.wait_ge(hid_lo, f)
                        cc.link(nc.vector.tensor_scalar(conv[:, :], pre[:, LEAD:], tap(LEAD), K["pc2"][:, ds(f + PC_FB, 1)], ALU.mult, ALU.add))
                        cc.link(nc.vector.scalar_tensor_tensor(conv[:, :], pre[:, 1:1 + L], tap(1), conv[:, :], ALU.mult, ALU.add))
                        nc.vector.scalar_tensor_tensor(conv[:, :], pre[:, 0:L], tap(0), conv[:, :], ALU.mult, ALU.add).then_inc(conv_done, 1)
                        if c == 1:
                            dve.wait_ge(down_hi, g + 1)
                            nc.vector.tensor_tensor(down["lo"][:, :, :], down_raw[:, :, :], down["hi"][:, :, :].bitcast(F32), ALU.subtract).then_inc(down_lo, 1)
                            if not last:
                                split(g + 1, 0, False)
                                split(g + 1, 1, False)
                        dve.wait_ge(silu, f + 1)
                        dve.wait_ge(in_mm, g * NPART + 2 * c + 2)
                        nc.vector.tensor_tensor(conv[:, :], ps_in[:, 1].rearrange("p a b -> p (a b)"), conv[:, :], ALU.mult).then_inc(hid_done, 1)
                        dve.wait_ge(hid_hi, f + 1)
                        nc.vector.tensor_tensor(hid["lo"][:, c], conv[:, :], hid["hi"][:, c].bitcast(F32), ALU.subtract).then_inc(hid_lo, 1)
                    cc.close()
                    for n in range(NOUT):
                        add(g, n)

                nc.vector.memset(pre[:, 0:LEAD], 0.0).then_inc(padded, 1)
                nm["vector"](dve, lambda: (split(0, 0, True), split(0, 1, True)))
                groups(dve, body)

            @block.tensor
            def _(pe):
                def project_half(q, half, ks=range(NK)):
                    for k in ks:
                        ins = product(nc, ps_in[:, q % 2, half], {p: w[p][:, q, k, :] for p in w},
                                      {p: hT[p][:, k, half * HALF:(half + 1) * HALF] for p in w}, k == 0, k == NK - 1)
                    return ins

                def project(g, q, first):
                    c, kind = q // 2, q % 2
                    pe.wait_ge(w_lo, g * NPART + q + 1)
                    if not first:
                        pe.wait_ge(hid_done if kind else evac, g * GF + c)
                    project_half(q, 0)
                    project_half(q, 1).then_inc(in_mm, 1)

                def body(g, first, last):
                    for q in range(2 if first else 1, NPART):
                        project(g, q, False)
                    if not last:
                        project(g + 1, 0, False)
                    pe.wait_ge(down_lo, g + 1)
                    share = lambda n, c: product(nc, ps_out[:, n % 4], {p: hid[p][:, c, n // 2 * P:(n // 2 + 1) * P] for p in w},
                                                 {p: down[p][:, c, (n % 2) * HALF:(n % 2 + 1) * HALF] for p in w}, c == 0, c == GF - 1)
                    pe.wait_ge(hid_lo, g * GF + 1)
                    for n in range(4):
                        if not first:
                            pe.wait_ge(added, g * NOUT + n - 3)
                        share(n, 0)
                    pe.wait_ge(hid_lo, (g + 1) * GF)
                    for n in range(4):
                        share(n, 1).then_inc(out_mm, 1)
                    for n in range(4, NOUT):
                        pe.wait_ge(added, g * NOUT + n - 3)
                        share(n, 0)
                        share(n, 1).then_inc(out_mm, 1)

                for t in range(NT):
                    nm["tensor"](pe, t)
                    if t == NT - 3:
                        pe.wait_ge(w_lo, 1)
                        pe.wait_ge(nm["lo_done"], NT // 2)
                        project_half(0, 0, range(NK // 2))
                    if t == NT - 2:
                        project_half(0, 0, range(NK // 2, NK))
                pe.wait_ge(w_lo, 2)
                project_half(1, 0)
                pe.wait_ge(nm["lo_done"], NT)
                project_half(0, 1).then_inc(in_mm, 1)
                project_half(1, 1).then_inc(in_mm, 1)
                groups(pe, body)


def build(nc, a, out):
    xbcT = nc.dram_tensor("xbcT_scratch", [XBC_W, L], F32, kind="Internal").ap()
    proj = nc.dram_tensor("proj_scratch", [L, SSM_W + QK_H * HD + KV_W], F32, kind="Internal").ap()
    y = nc.dram_tensor("y_scratch", [L, SSM_W], F32, kind="Internal").ap()
    x_new = nc.dram_tensor("x_new_scratch", [L, D], F32, kind="Internal").ap()
    with ExitStack() as ctx:
        keep = Room(nc, ctx, "keep")
        K = constant_tiles(keep)
        with ExitStack() as first:
            r = Room(nc, first, "in")
            S = {n: r.sb(n, [P, NT, SSM_H]) for n in ("dt", "dA", "nacs", "eacs", "cdec", "wend")}
            hT = {part: r.sb(f"hT_{part}", [P, NK, L], F32R) for part in ("hi", "lo")}
            scan_stage(nc, a, K, hT, xbcT, S, proj, y)
        rstd = keep.sb("rstd", [P, NT])
        mix_stage(nc, a, K, proj, y, x_new, rstd)
        with ExitStack() as second:
            r = Room(nc, second, "up")
            hT = {part: r.sb(f"hT_{part}", [P, NK, L], F32R) for part in ("hi", "lo")}
            x_sb = r.sb("x_sb", [P, NT, D])
            ffn_stage(nc, a, K, hT, x_sb, x_new, rstd, out.rearrange("o t d -> (o t) d"))


_INS = ['x', 'positions', 'norm_mix', 'w_in', 'conv_w', 'conv_b', 'dt_bias', 'a_log', 'd_skip', 'ssm_norm',
        'q_norm', 'k_norm', 'sinks', 'w_out', 'norm_ffn', 'w_ffn_in', 'ffn_conv_w', 'ffn_conv_b', 'w_ffn_out']


def kernel(**inputs):
    import concourse.bacc as _bacc
    from concourse.bass_utils import run_bass_kernel_spmd as _run

    nc = _bacc.Bacc("TRN2", target_bir_lowering=False, num_devices=1)
    arrays, args = {}, {}
    for name in _INS:
        v = np.ascontiguousarray(inputs[name])
        arrays[f"in_{name}"] = v
        args[name] = nc.dram_tensor(f"in_{name}", v.shape, mybir.dt.from_np(v.dtype), kind="ExternalInput").ap()
    out = nc.dram_tensor("out_x", [1, L, D], F32, kind="ExternalOutput").ap()
    build(nc, args, out)
    r = _run(nc, [arrays], core_ids=[0])
    return r.results[0]["out_x"]
```
